# Optimizing a Trainium2 kernel written in Bass

```python
import math
import jax, jax.numpy as jnp
from jax import lax
import numpy as np

D_MODEL = 2048
BATCH = 1
SEQ = 256
DEPTH = 2

CHUNK = 64
D_MIX = D_MODEL
N_MIXERS = 4
GROUP_W = D_MIX // N_MIXERS
LRU_HEADS = 4
LRU_BLOCK = GROUP_W // LRU_HEADS
LRU_CONV = 4
LRU_C = 8.0
SCONV_W = 3
GLA_HEADS = 4
GLA_DK = GROUP_W // (2 * GLA_HEADS)
GLA_DV = GROUP_W // GLA_HEADS
GLA_RANK = 16
GLA_TAU = 16.0
ATT_HEADS = 4
ATT_HD = GROUP_W // ATT_HEADS
ATT_PREV_CHUNKS = 8
ATT_BAND = ATT_PREV_CHUNKS + 1
REL_CLIP = 256
N_GROUPS = 4
EXPERTS_PER_GROUP = 4
N_EXPERTS = N_GROUPS * EXPERTS_PER_GROUP
TOP_K = 2
D_EXPERT = D_MODEL // 4
LN_EPS = 1e-5
RMS_EPS = 1e-6
DN_ALPHA = (2 * DEPTH) ** 0.25
DN_BETA = (8 * DEPTH) ** -0.25

IN_SPLITS = (GROUP_W, GROUP_W,
             GROUP_W, GROUP_W, GROUP_W,
             GLA_HEADS * GLA_DK, GLA_HEADS * GLA_DK, GROUP_W, GROUP_W, GLA_RANK,
             GROUP_W, GROUP_W, GROUP_W)
D_IN = sum(IN_SPLITS)
SPLIT_POINTS = tuple(int(p) for p in np.cumsum(IN_SPLITS)[:-1])

kernel_name = 'hybrid_parallel_mixers_hier_moe_deepnorm'

def layer_norm(x, g, b):
    xf = x.astype(jnp.float32)
    mu = jnp.mean(xf, -1, keepdims=True)
    var = jnp.mean(jnp.square(xf - mu), -1, keepdims=True)
    return ((xf - mu) * lax.rsqrt(var + LN_EPS)).astype(x.dtype) * g + b

def causal_dwconv(x, w):
    k, c = w.shape
    return lax.conv_general_dilated(x, w[:, None, :].astype(x.dtype), window_strides=(1,),
                                    padding=[(k - 1, 0)],
                                    dimension_numbers=('NWC', 'WIO', 'NWC'),
                                    feature_group_count=c)

def rg_lru(u, w_a, b_a, w_x, b_x, lam):
    bn, s, _ = u.shape
    ub = u.reshape(bn, s, LRU_HEADS, LRU_BLOCK)
    r = jax.nn.sigmoid(jnp.einsum('bshi,hij->bshj', ub, w_a).reshape(bn, s, GROUP_W) + b_a)
    i = jax.nn.sigmoid(jnp.einsum('bshi,hij->bshj', ub, w_x).reshape(bn, s, GROUP_W) + b_x)
    log_a = (-LRU_C * r.astype(jnp.float32)) * jax.nn.softplus(-lam.astype(jnp.float32))
    a = jnp.exp(log_a)
    mult = jnp.sqrt(-jnp.expm1(2.0 * log_a))
    bterm = mult * (i * u).astype(jnp.float32)

    def combine(c1, c2):
        a1, b1 = c1
        a2, b2 = c2
        return a1 * a2, a2 * b1 + b2

    _, h = lax.associative_scan(combine, (a, bterm), axis=1)
    return h.astype(u.dtype)

def gla(q, k, v, g, a_lr, w_a2, b_a2, norm_w):
    f32 = jnp.float32
    bn, s, _ = q.shape
    nc = s // CHUNK
    q = q.reshape(bn, nc, CHUNK, GLA_HEADS, GLA_DK).astype(f32) * (GLA_DK ** -0.5)
    k = k.reshape(bn, nc, CHUNK, GLA_HEADS, GLA_DK).astype(f32)
    v = v.reshape(bn, nc, CHUNK, GLA_HEADS, GLA_DV).astype(f32)
    log_alpha = jax.nn.log_sigmoid((a_lr @ w_a2 + b_a2).astype(f32)) / GLA_TAU
    log_alpha = log_alpha.reshape(bn, nc, CHUNK, GLA_HEADS, GLA_DK)
    bcum = jnp.cumsum(log_alpha, axis=2)
    b_last = bcum[:, :, -1]
    q_dec = q * jnp.exp(bcum)
    k_inv = k * jnp.exp(-bcum)
    k_end = k * jnp.exp(b_last[:, :, None] - bcum)
    scores = jnp.einsum('bnthk,bnshk->bnhts', q_dec, k_inv)
    causal = jnp.tril(jnp.ones((CHUNK, CHUNK), dtype=bool))
    scores = jnp.where(causal, scores, 0.0)
    o_intra = jnp.einsum('bnhts,bnshv->bnthv', scores, v)
    chunk_kv = jnp.einsum('bnshk,bnshv->nbhkv', k_end, v)
    decay = jnp.exp(b_last).transpose(1, 0, 2, 3)

    def step(state, inp):
        d, kv = inp
        return state * d[..., None] + kv, state

    s0 = jnp.zeros((bn, GLA_HEADS, GLA_DK, GLA_DV), f32)
    _, prev = lax.scan(step, s0, (decay, chunk_kv))
    o_inter = jnp.einsum('bnthk,nbhkv->bnthv', q_dec, prev)
    o = o_intra + o_inter
    o = o * lax.rsqrt(jnp.mean(o * o, -1, keepdims=True) + RMS_EPS)
    o = o.reshape(bn, s, GROUP_W).astype(g.dtype) * norm_w
    return o * jax.nn.silu(g)

def chunk_local_attention(q, k, v, rel_bias):
    f32 = jnp.float32
    bn, s, _ = q.shape
    nc = s // CHUNK
    q = q.reshape(bn, nc, CHUNK, ATT_HEADS, ATT_HD)
    k = k.reshape(bn, nc, CHUNK, ATT_HEADS, ATT_HD)
    v = v.reshape(bn, nc, CHUNK, ATT_HEADS, ATT_HD)
    pad = ((0, 0), (ATT_PREV_CHUNKS, 0), (0, 0), (0, 0), (0, 0))
    kp = jnp.pad(k, pad)
    vp = jnp.pad(v, pad)
    band_idx = jnp.arange(nc)[:, None] + jnp.arange(ATT_BAND)[None, :]
    kb = kp[:, band_idx].reshape(bn, nc, ATT_BAND * CHUNK, ATT_HEADS, ATT_HD)
    vb = vp[:, band_idx].reshape(bn, nc, ATT_BAND * CHUNK, ATT_HEADS, ATT_HD)
    scores = jnp.einsum('bnqhd,bnkhd->bnhqk', q, kb).astype(f32) * (ATT_HD ** -0.5)
    qpos = jnp.arange(CHUNK)
    kpos = jnp.arange(ATT_BAND * CHUNK) - ATT_PREV_CHUNKS * CHUNK
    rel_idx = jnp.clip(qpos[:, None] - kpos[None, :], -REL_CLIP, REL_CLIP) + REL_CLIP
    bias = rel_bias[:, rel_idx].astype(f32)
    valid = (jnp.arange(nc)[:, None] - ATT_PREV_CHUNKS + jnp.arange(ATT_BAND)[None, :]) >= 0
    valid = jnp.repeat(valid, CHUNK, axis=1)
    scores = jnp.where(valid[None, :, None, None, :], scores + bias, -jnp.inf)
    p = jax.nn.softmax(scores, axis=-1).astype(v.dtype)
    o = jnp.einsum('bnhqk,bnkhd->bnqhd', p, vb)
    return o.reshape(bn, s, GROUP_W)

def hier_moe(x, w_rg, b_rg, w_re, b_re, w_gate, w_up, w_down):
    f32 = jnp.float32
    bn, s, d = x.shape
    xt = x.reshape(-1, d)
    g_prob = jax.nn.softmax((xt @ w_rg).astype(f32) + b_rg.astype(f32), axis=-1)
    g_val, g_idx = lax.top_k(g_prob, 1)
    e_logits = ((xt @ w_re).astype(f32) + b_re.astype(f32)).reshape(-1, N_GROUPS, EXPERTS_PER_GROUP)
    g_onehot = jax.nn.one_hot(g_idx[:, 0], N_GROUPS, dtype=f32)
    e_in_group = jnp.einsum('tg,tge->te', g_onehot, e_logits)
    e_val, e_loc = lax.top_k(e_in_group, TOP_K)
    e_w = jax.nn.softmax(e_val, axis=-1) * g_val
    e_idx = g_idx * EXPERTS_PER_GROUP + e_loc
    combine = jnp.sum(jax.nn.one_hot(e_idx, N_EXPERTS, dtype=f32) * e_w[..., None], axis=1)
    combine = combine.astype(x.dtype)
    out = jnp.zeros_like(xt)
    for e in range(N_EXPERTS):
        h = jax.nn.silu(xt @ w_gate[e]) * (xt @ w_up[e])
        out = out + combine[:, e:e + 1] * (h @ w_down[e])
    return out.reshape(bn, s, d)

def setup_inputs(seed: int = 0) -> dict:
    key = jax.random.key(seed)
    ks = jax.random.split(key, 32)
    f32 = jnp.float32
    L = DEPTH

    def nrm(k, shape, scale):
        return jax.random.normal(k, shape, f32) * scale

    a_c = jax.random.uniform(ks[9], (L, GROUP_W), f32, 0.9, 0.999)
    a_base = a_c ** (1.0 / LRU_C)
    lru_lam = jnp.log(a_base) - jnp.log1p(-a_base)
    return {
        'x': nrm(ks[0], (BATCH, SEQ, D_MODEL), 1.0),
        'ln0_g': 1.0 + nrm(ks[1], (D_MODEL,), 0.02),
        'ln0_b': nrm(ks[2], (D_MODEL,), 0.02),
        'w_in': nrm(ks[3], (L, D_MODEL, D_IN), D_MODEL ** -0.5),
        'conv_a_w': nrm(ks[4], (L, LRU_CONV, GROUP_W), LRU_CONV ** -0.5),
        'conv_a_b': nrm(ks[5], (L, GROUP_W), 0.02),
        'lru_wa': nrm(ks[6], (L, LRU_HEADS, LRU_BLOCK, LRU_BLOCK), LRU_BLOCK ** -0.5),
        'lru_ba': nrm(ks[7], (L, GROUP_W), 0.02),
        'lru_wx': nrm(ks[8], (L, LRU_HEADS, LRU_BLOCK, LRU_BLOCK), LRU_BLOCK ** -0.5),
        'lru_bx': nrm(ks[10], (L, GROUP_W), 0.02),
        'lru_lam': lru_lam,
        'conv_b_w': nrm(ks[11], (L, SCONV_W, GROUP_W), SCONV_W ** -0.5),
        'gla_wa2': nrm(ks[12], (L, GLA_RANK, GLA_HEADS * GLA_DK), GLA_RANK ** -0.5),
        'gla_ba2': nrm(ks[13], (L, GLA_HEADS * GLA_DK), 0.02),
        'gla_norm_w': 1.0 + nrm(ks[14], (L, GROUP_W), 0.02),
        'att_rel_bias': nrm(ks[15], (L, ATT_HEADS, 2 * REL_CLIP + 1), 0.1),
        'w_out': nrm(ks[16], (L, D_MIX, D_MODEL), DN_BETA * D_MIX ** -0.5),
        'ln1_g': 1.0 + nrm(ks[17], (L, D_MODEL), 0.02),
        'ln1_b': nrm(ks[18], (L, D_MODEL), 0.02),
        'w_rg': nrm(ks[19], (L, D_MODEL, N_GROUPS), D_MODEL ** -0.5),
        'b_rg': nrm(ks[20], (L, N_GROUPS), 0.01),
        'w_re': nrm(ks[21], (L, D_MODEL, N_EXPERTS), D_MODEL ** -0.5),
        'b_re': nrm(ks[22], (L, N_EXPERTS), 0.01),
        'w_gate': nrm(ks[23], (L, N_EXPERTS, D_MODEL, D_EXPERT), D_MODEL ** -0.5),
        'w_up': nrm(ks[24], (L, N_EXPERTS, D_MODEL, D_EXPERT), D_MODEL ** -0.5),
        'w_down': nrm(ks[25], (L, N_EXPERTS, D_EXPERT, D_MODEL), DN_BETA * D_EXPERT ** -0.5),
        'ln2_g': 1.0 + nrm(ks[26], (L, D_MODEL), 0.02),
        'ln2_b': nrm(ks[27], (L, D_MODEL), 0.02),
    }

def reference(x, ln0_g, ln0_b, w_in, conv_a_w, conv_a_b, lru_wa, lru_ba, lru_wx, lru_bx, lru_lam,
              conv_b_w, gla_wa2, gla_ba2, gla_norm_w, att_rel_bias, w_out, ln1_g, ln1_b,
              w_rg, b_rg, w_re, b_re, w_gate, w_up, w_down, ln2_g, ln2_b):
    h = layer_norm(x, ln0_g, ln0_b)
    for l in range(DEPTH):
        z = h @ w_in[l]
        (a_x, a_g, b_b, b_c, b_h, c_q, c_k, c_v, c_g, c_a, d_q, d_k, d_v) = jnp.split(z, SPLIT_POINTS, axis=-1)
        u = causal_dwconv(a_x, conv_a_w[l]) + conv_a_b[l]
        y_a = rg_lru(u, lru_wa[l], lru_ba[l], lru_wx[l], lru_bx[l], lru_lam[l]) * jax.nn.gelu(a_g)
        y_b = b_b * causal_dwconv(b_c * b_h, conv_b_w[l])
        y_c = gla(c_q, c_k, c_v, c_g, c_a, gla_wa2[l], gla_ba2[l], gla_norm_w[l])
        y_d = chunk_local_attention(d_q, d_k, d_v, att_rel_bias[l])
        mix = jnp.concatenate([y_a, y_b, y_c, y_d], axis=-1) @ w_out[l]
        h = layer_norm(DN_ALPHA * h + mix, ln1_g[l], ln1_b[l])
        ffn = hier_moe(h, w_rg[l], b_rg[l], w_re[l], b_re[l], w_gate[l], w_up[l], w_down[l])
        h = layer_norm(DN_ALPHA * h + ffn, ln2_g[l], ln2_b[l])
    return h


_drawn_inputs = setup_inputs


def setup_inputs(seed=0):
    import zlib

    import numpy as np

    out = dict(_drawn_inputs(seed))
    spreads = {}
    factors = {'conv_a_b': 3.297,
     'lru_ba': 64.0,
     'lru_bx': 59.693,
     'gla_wa2': 3.016,
     'gla_ba2': 8.0,
     'gla_norm_w': 8.0,
     'att_rel_bias': 8.0,
     'b_rg': 8.0,
     'b_re': 25.691}
    for name, (base, spread) in spreads.items():
        noise = np.random.default_rng([zlib.crc32(name.encode()), seed]).standard_normal(out[name].shape)
        drawn = base * np.exp(spread * noise) if base else spread * noise
        out[name] = __import__('jax').numpy.asarray(drawn.astype(out[name].dtype))
    for name, factor in factors.items():
        out[name] = (out[name] * factor).astype(out[name].dtype)
    return out
```

```python
from contextlib import ExitStack

import numpy as np
import concourse.bass as bass
from concourse import mybir

F32 = mybir.dt.float32
I32 = mybir.dt.int32
U32 = mybir.dt.uint32
ALU = mybir.AluOpType
ACT = mybir.ActivationFunctionType
AX = mybir.AxisListType

P = 128
BLK = 64
KB = 256
SLOTS = 3
HALVES = 2 * SLOTS
BIG = 3.0e38
NEG = -1.0e30

W_IN = [("dq", 4112), ("dk", 4624), ("dv", 5136), ("cqk", 2560), ("cv", 3072), ("cg", 3584),
        ("ax", 0), ("ag", 512), ("bc", 1536), ("bh", 2048), ("bb", 1024)]
C_A = 4096
RANK = 16

ROWS = {"conv_a_w": (0, 16), "conv_a_b": (16, 4), "lru_ba": (20, 4), "lru_bx": (24, 4), "lru_lam": (28, 4),
        "conv_b_w": (32, 12), "gla_ba2": (44, 2), "gla_norm_w": (46, 4)}
NROWS = 50


class Signal:

    def __init__(self, sem, per_layer):
        self.sem, self.per_layer = sem, per_layer

    def at(self, layer, k):
        return layer * self.per_layer + k


def trunk(nc, x, ln0_g, ln0_b, w_in, conv_a_w, conv_a_b, lru_wa, lru_ba, lru_wx, lru_bx, lru_lam, conv_b_w,
          gla_wa2, gla_ba2, gla_norm_w, att_rel_bias, w_out, ln1_g, ln1_b, w_rg, b_rg, w_re, b_re,
          w_gate, w_up, w_down, ln2_g, ln2_b, out):
    _, T, D = x.shape
    L, E = w_gate.shape[0], w_gate.shape[1]
    F = w_gate.shape[3]
    KD = D // P
    KF = F // P
    NT = T // P
    CH = 64
    NC = T // CH
    HEADS = 4
    G = w_rg.shape[2]
    NR = G + E
    S = 2 * T
    SP_ = S + BLK
    N_IN = len(W_IN)
    N_OUT = D // 512
    FIRST_E = N_IN + N_OUT
    PER_SLOT = (FIRST_E + 3 * E) // SLOTS
    assert (FIRST_E + 3 * E) % SLOTS == 0 and FIRST_E % SLOTS == 0 and T == 256 and D == 2048 and F == 512
    ALPHA = float((2 * L) ** 0.25)
    LN_EPS, RMS_EPS = 1e-5, 1e-6
    LRU_C, TAU = 8.0, 16.0

    ctx = ExitStack()
    with ctx:
        def sb(name, shape, dt=F32):
            return ctx.enter_context(nc.sbuf_tensor(name, shape, dt))

        def semaphore(name):
            return ctx.enter_context(nc.semaphore(name))

        def signal(name, per_layer):
            return Signal(semaphore(name), per_layer)

        ring = sb("ring", [P, SLOTS, KD * 512])
        h = sb("h", [P, NT, D])
        arena = sb("arena", [P, 88 * KB])

        def area(kib, words):
            return arena[:, kib * KB:kib * KB + words]

        def unit(kib):
            return area(kib, 1024)

        def blocks(ap, n):
            return ap.rearrange("p (b t) -> p b t", b=n)

        hT = area(0, KD * T).rearrange("p (k t) -> p k t", k=KD)
        mixT = area(16, KD * T).rearrange("p (k t) -> p k t", k=KD)
        a_qT, a_kT, a_v, a_H = unit(32), unit(36), unit(40), unit(44)
        a_P = blocks(area(48, HEADS * 384), HEADS)
        a_PT = blocks(area(54, HEADS * 384), HEADS)
        c_qk, c_v, c_g = unit(60), unit(64), unit(68)
        c_bcum, c_t1 = area(72, 512), area(74, 512)
        c_qd, c_ki, c_ke = area(76, 512), area(78, 512), area(80, 512)
        c_aT = area(82, T)[0:RANK, :]
        c_wa2 = area(83, 256)[0:RANK, :]
        c_wca = area(84, KD * RANK).rearrange("p (k r) -> p k r", k=KD)
        c_keT = area(86, 512).rearrange("p (t c) -> p t c", t=NT)
        c_scT = blocks(unit(32), 8)
        c_state = area(36, 3 * 256).rearrange("p (n b v) -> p n b v", n=3, b=2)
        c_sq, c_rs = unit(44), unit(48)
        r_x, r_g, r_u, r_r, r_i = unit(52), unit(56), unit(60), unit(40), unit(76)
        r_w = area(80, 1024).rearrange("p (m h j) -> p m h j", m=2, h=HEADS)
        r_t = unit(32)
        b_c, b_h, b_cv, b_p = unit(64), unit(68), unit(72), unit(36)
        gb1 = area(72, 2 * D).rearrange("p (m n) -> p m n", m=2)
        xgT = area(0, KD * SP_).rearrange("p (k s) -> p k s", k=KD)
        yT = area(36, KD * SP_).rearrange("p (k s) -> p k s", k=KD)
        ySort = area(0, 4 * D).rearrange("p (b n) -> p b n", b=4)
        hot = area(36, 2 * S).rearrange("p (t s) -> p t s", t=NT)
        hotw = area(40, 2 * S).rearrange("p (t s) -> p t s", t=NT)
        xe = area(72, KD * BLK).rearrange("p (k s) -> p k s", k=KD)
        hmid, sgate = area(76, 256), area(77, 256)
        hmT = area(82, 2 * P).rearrange("p (q n) -> p q n", q=2)
        yraw = area(83, 1024)
        pw = area(78, 4 * T).rearrange("p (b t) -> p b t", b=4)
        gb2 = area(56, 2 * D).rearrange("p (m n) -> p m n", m=2)
        par_rows = area(32, P)
        ident, ones, before, anti = sb("ident", [P, P]), sb("ones", [P, P]), sb("before", [P, P]), sb("anti", [P, P])
        causal = sb("causal", [P, P])
        lo_row, hi_row = sb("lo_row", [1, P]), sb("hi_row", [1, P])
        par = sb("par", [P, L, NROWS])
        cs, csn = sb("cs", [P, L, 4]), sb("csn", [P, L, 4])
        cur, cur_cs = sb("cur", [P, NROWS]), sb("cur_cs", [P, 2, 4])
        cur_ln = sb("cur_ln", [P, 2, 2, KD])
        sp = sb("sp", [P, 4, L * 4])
        lnc = sb("lnc", [P, 1 + 2 * L, 2, KD])
        wr = area(52, KD * NR).rearrange("p (k n) -> p k n", k=KD)
        br = area(54, NR)
        desc = sb("desc", [P, 4])
        slot_iota = sb("slot_iota", [P, S], mybir.dt.int16)
        stats = sb("stats", [P, NT, 4, 6])
        mv = sb("mv", [P, NT, 2])
        rstd = sb("rstd", [P, NT, 2])
        nmax, rsum = sb("nmax", [P, 2, HEADS]), sb("rsum", [P, 2, HEADS])
        blast = sb("blast", [P, 8])
        def small(at, shape):
            n = int(np.prod(shape))
            ap = arena[:, 48 * KB + at:48 * KB + at + n]
            if len(shape) == 2:
                return ap.rearrange("p (a b) -> p a b", b=shape[1])
            return ap.rearrange("p (a b c) -> p a b c", b=shape[1], c=shape[2])

        lg = small(0, (NT, NR))
        gmax, rk, rkm, goh = small(64, (NT, 1)), small(72, (NT, 4)), small(80, (NT, 1)), small(88, (NT, 4))
        t16, eg, oh = small(96, (NT, 16)), small(128, (NT, 4)), small(136, (2, NT, 4))
        emax = small(152, (2, NT, 1))
        ex = small(160, (NT, 5))
        gval, wts = small(176, (NT, 1)), small(184, (2, NT, 1))
        M = small(192, (3, NT, 16))
        pos, pos12 = small(320, (NT, 16)), small(352, (2, NT, 1))
        tab = small(384, (3, 16))
        scn = small(448, (2, 16))
        carry = sb("carry", [P, 1])
        tabi = sb("tabi", [P, 4, 16], I32)

        ps = ctx.enter_context(nc.psum_tensor("ps", [P, 8, 512], F32))

        def banks(b, n):
            return ps[:, b:b + n, :].rearrange("p b n -> p (b n)")

        def slab(slot):
            return ring[:, slot, :].rearrange("p (k n) -> p k n", k=KD)

        def slab_down(slot):
            return ring[:, slot, :].rearrange("p (k n) -> p k n", k=KF)

        slab_loaded = [[semaphore(f"slab_loaded_{s}{i}") for i in range(2)] for s in range(SLOTS)]
        half_used = semaphore("half_used")
        x_loaded, par_loaded, lnc_loaded = semaphore("x_loaded"), semaphore("par_loaded"), semaphore("lnc_loaded")
        small_loaded = signal("small_loaded", 16 * 3)
        router_loaded = signal("router_loaded", 16 * 4)
        lru_loaded = signal("lru_loaded", 16 * 2)
        gb0_loaded = semaphore("gb0_loaded")
        gb1_loaded, gb2_loaded = signal("gb1_loaded", 32), signal("gb2_loaded", 32)
        stored = semaphore("stored")
        consts = semaphore("consts")
        par_T, par_ready = semaphore("par_T"), semaphore("par_ready")
        sp_in, sp_exp, cs_ready = semaphore("sp_in"), semaphore("sp_exp"), semaphore("cs_ready")
        var_ready, std_ready, xn_ready = (semaphore(n) for n in ("var_ready", "std_ready", "xn_ready"))
        xnT_done, hT_act, hT_dve = (semaphore(n) for n in ("xnT_done", "hT_act", "hT_dve"))
        h_ready = semaphore("h_ready")
        acc_full = signal("acc_full", 2 * (N_IN + N_OUT))
        z_evac = signal("z_evac", 2 * (N_IN - 1))
        res_add = signal("res_add", 2 * N_OUT)
        att_scores, att_max, att_exp, att_prob = (signal(n, 1) for n in ("att_scores", "att_max", "att_exp", "att_prob"))
        att_pT, att_pTs, att_o, att_done = (signal(n, 1) for n in ("att_pT", "att_pTs", "att_o", "att_done"))
        ca_done, ca_evac, la_done, la_abs, la_ln, bc_ready = (
            signal(n, 1) for n in ("ca_done", "ca_evac", "la_done", "la_abs", "la_ln", "bc_ready"))
        exps_ready, qk_ready, bl_ready, dec_ready = (signal(n, 1) for n in ("exps_ready", "qk_ready", "bl_ready", "dec_ready"))
        ke_T, ke_evac, gsc_done, gsc_evac = (signal(n, 1) for n in ("ke_T", "ke_evac", "gsc_done", "gsc_evac"))
        kv_done, state_ready, go_done, sq_ready, ms_done, ms_sqrt, gla_done = (
            signal(n, 1) for n in ("kv_done", "state_ready", "go_done", "sq_ready", "ms_done", "ms_sqrt", "gla_done"))
        u_ready, gates_done, sig_ready, at_ready, om_ready, mult_ready, lru_done, gates_free = (
            signal(n, 1) for n in ("u_ready", "gates_done", "sig_ready", "at_ready", "om_ready", "mult_ready",
                                   "lru_done", "gates_free"))
        mixb_ready = signal("mixb_ready", 2)
        logits_done, ex_in, ex_ready, m_ready, ranks_done, tab_ready, hot_ready = (
            signal(n, 1) for n in ("logits_done", "ex_in", "ex_ready", "m_ready", "ranks_done", "tab_ready", "hot_ready"))
        pwT_done, pw_ready = (signal(n, 1) for n in ("pwT_done", "pw_ready"))
        cur_ready = semaphore("cur_ready")
        gath_done = signal("gath_done", KD)
        gath_act, gath_dve = signal("gath_act", KD // 2), signal("gath_dve", KD // 2)
        xe_ready, gu_done, sg_ready, hm_ready, hmT_done, hmT_ready, y_done, yraw_ready, yt_done, y_evac = (
            semaphore(n) for n in ("xe_ready", "gu_done", "sg_ready", "hm_ready", "hmT_done", "hmT_ready", "y_done",
                                   "yraw_ready", "yt_done", "y_evac"))
        yS_done = signal("yS_done", 16)
        yS_act, yS_dve = signal("yS_act", 8), signal("yS_dve", 8)
        sc_done, ffn_add = signal("sc_done", 2 * N_OUT), signal("ffn_add", 2 * N_OUT)

        block = ctx.enter_context(nc.Block())

        def expert_row(eng, row, e):
            hi = {0: S, 1: T // BLK, 2: 4096}[row]
            return eng.value_load(tabi[0:1, row, bass.ds(e, 1)], min_val=1 if row == 1 else 0, max_val=hi)

        def bank_order(head):
            return (head % 2) * 2 + head // 2

        def block_start(first, j):
            return nc.s_assert_within(first + j * BLK, 0, S, skip_runtime_bounds_check_because=
                                      "a block starts at or before its expert's last slot")

        @block.sync
        def _(sp_eng):
            eng = sp_eng

            def load(l, slab_index, slot, halves):
                eng.wait_ge(half_used, l * (2 * (FIRST_E + 3 * E)) + (2 * slab_index + 2))
                for i, (dst, src) in enumerate(halves):
                    eng.dma_start(dst, src()).then_inc(slab_loaded[slot][i], 16)

            eng.dma_start(h[:], x[0].rearrange("(t p) n -> p t n", p=P)).then_inc(x_loaded, 16)
            with eng.Fori(0, L) as l:
                for s, (_, c0) in enumerate(W_IN):
                    src = w_in[bass.ds(l, 1), :, c0:c0 + 512].rearrange("o (p k) n -> p (o k) n", k=KD)
                    eng.wait_ge(half_used, l * (2 * (FIRST_E + 3 * E)) + max(2 * s + 2, 4))
                    for i in (1, 0):
                        eng.dma_start(slab(s % SLOTS)[:, 8 * i:8 * i + 8, :], src[:, 8 * i:8 * i + 8, :]
                                      ).then_inc(slab_loaded[s % SLOTS][i], 16)
                for c in range(N_OUT):
                    s = N_IN + c
                    src = w_out[bass.ds(l, 1), :, c * 512:c * 512 + 512].rearrange("o (k p) n -> p (o k) n", p=P)
                    load(l, s, s % SLOTS, [(slab(s % SLOTS)[:, 8 * i:8 * i + 8, :], lambda i=i: src[:, 8 * i:8 * i + 8, :])
                                           for i in range(2)])
                with eng.Fori(0, E) as e:
                    eng.wait_ge(half_used, l * (2 * (FIRST_E + 3 * E)) + 2 * (FIRST_E + 3 * e + 1) + 2)
                    for i in range(2):
                        for m, w in enumerate((w_gate, w_up)):
                            src = w.rearrange("l e d f -> (l e) d f")[bass.ds(l * E + e, 1)].rearrange(
                                "o (p k) n -> p (o k) n", k=KD)
                            eng.dma_start(slab(m)[:, 8 * i:8 * i + 8, :], src[:, 8 * i:8 * i + 8, :]
                                          ).then_inc(slab_loaded[m][i], 16)
                    src = w_down.rearrange("l e f d -> (l e) f d")[bass.ds(l * E + e, 1)].rearrange(
                        "o (k p) n -> p (o k) n", p=P)
                    load(l, FIRST_E + 3 * e + 2, 2, [(slab_down(2)[:, 2 * i:2 * i + 2, :], lambda i=i: src[:, 2 * i:2 * i + 2, :])
                                                     for i in range(2)])
            eng.wait_ge(h_ready, NT * (1 + 2 * L))
            eng.dma_start(out[0].rearrange("(t p) n -> p t n", p=P), h[:]).then_inc(stored, 16)
            eng.wait_ge(stored, 16)

        @block.gpsimd
        def _(eng):
            for t in (ident, before, anti, lo_row, hi_row):
                eng.memset(t[:], 0.0)
            eng.memset(causal[:], 1.0)
            eng.memset(ones[:], 1.0)
            eng.memset(carry[:], 0.0)
            eng.drain()
            eng.memset(lo_row[:, 0:CH], NEG)
            eng.memset(hi_row[:, CH:P], 1.0)
            eng.affine_select(out=ident[:], in_=ident[:], compare_op=ALU.not_equal, fill=1.0, base=0,
                              pattern=[[-1, P]], channel_multiplier=1)
            eng.affine_select(out=anti[:], in_=anti[:], compare_op=ALU.not_equal, fill=1.0, base=-(P - 1),
                              pattern=[[1, P]], channel_multiplier=1)
            eng.affine_select(out=before[:], in_=before[:], compare_op=ALU.is_ge, fill=1.0, base=0,
                              pattern=[[-1, P]], channel_multiplier=1)
            eng.affine_select(out=causal[:], in_=causal[:], compare_op=ALU.is_ge, fill=0.0, base=0,
                              pattern=[[1, P]], channel_multiplier=-1)
            eng.iota(slot_iota[:], pattern=[[1, S]], base=0, channel_multiplier=0,
                     allow_small_or_imprecise_dtypes=True)
            eng.iota(desc[:], pattern=[[-1, 4]], base=4, channel_multiplier=0,
                     allow_small_or_imprecise_dtypes=True)
            eng.drain()
            eng.affine_select(out=causal[:, CH:P], in_=causal[:, CH:P], compare_op=ALU.is_ge, fill=0.0, base=-CH,
                              pattern=[[0, CH]], channel_multiplier=1).then_inc(consts, 1)

            def affine_h(gb_loaded, gb_value, gb, read_done, read_value, before_last=()):
                eng.wait_ge(gb_loaded, gb_value)
                eng.wait_ge(read_done, read_value)
                for t in range(NT):
                    eng.tensor_tensor(h[:, t, :], h[:, t, :], gb[:, 0, :], ALU.mult)
                eng.drain()
                for sem, value in before_last:
                    eng.wait_ge(sem, value)
                for t in range(NT):
                    eng.tensor_tensor(h[:, t, :], h[:, t, :], gb[:, 1, :], ALU.add).then_inc(h_ready, 1)

            affine_h(gb0_loaded, 32, gb2, xnT_done, 8)
            with eng.Fori(0, L) as l:
                affine_h(gb1_loaded.sem, gb1_loaded.at(l, 32), gb1, gath_done.sem, gath_done.at(l, KD),
                         ((gath_act.sem, gath_act.at(l, KD // 2)), (gath_dve.sem, gath_dve.at(l, KD // 2)),
                          (tab_ready.sem, tab_ready.at(l, 1))))
                eng.drain()
                with eng.Fori(0, E) as e:
                    first, n, g0 = expert_row(eng, 0, e), expert_row(eng, 1, e), expert_row(eng, 2, e)
                    with eng.Fori(0, n) as j:
                        eng.wait_ge(gu_done, g0 + j + 1)
                        eng.tensor_copy(xe, xgT[:, :, bass.ds(block_start(first, j), BLK)]).then_inc(xe_ready, 1)
                affine_h(gb2_loaded.sem, gb2_loaded.at(l, 32), gb2, xnT_done, (2 * l + 3) * 8)

        def norm_T_dyn(eng, l, second):
            eng.wait_ge(var_ready, 2 * l + 2 + second)
            eng.activation(rstd[:, :, 0], rstd[:, :, 1], ACT.Sqrt).then_inc(std_ready, 1)
            for c in range(0, 8, 2):
                eng.wait_ge(xnT_done, (2 * l + 1 + second) * 8 + c + 1)
                for k in (2 * c, 2 * c + 1):
                    last = eng.activation(hT[:, k, :], ps[:, c, (k % 2) * T:(k % 2) * T + T], ACT.Identity,
                                          bias=cur_ln[:, second, 1, k:k + 1],
                                          scale=cur_ln[:, second, 0, k:k + 1])
                last.then_inc(hT_act, 1)

        @block.scalar
        def _(eng):
            for l in range(L):
                for name, ap in (("conv_a_w", conv_a_w), ("conv_b_w", conv_b_w)):
                    r0, n = ROWS[name]
                    eng.dma_start(par_rows[l * NROWS + r0:l * NROWS + r0 + n, :],
                                  ap[l].rearrange("k (b c) -> (k b) c", c=P)).then_inc(par_loaded, 16)
                for name, ap in (("conv_a_b", conv_a_b), ("lru_ba", lru_ba), ("lru_bx", lru_bx), ("lru_lam", lru_lam),
                                 ("gla_ba2", gla_ba2), ("gla_norm_w", gla_norm_w)):
                    r0, n = ROWS[name]
                    eng.dma_start(par_rows[l * NROWS + r0:l * NROWS + r0 + n, :],
                                  ap[l].rearrange("(b c) -> b c", c=P)).then_inc(par_loaded, 16)
            vectors = [(ln0_g, ln0_b)]
            for l in range(L):
                vectors += [(ln1_g[l], ln1_b[l]), (ln2_g[l], ln2_b[l])]
            for n, pair in enumerate(vectors):
                for m, v in enumerate(pair):
                    eng.dma_start(lnc[:, n, m, :], v.rearrange("(p k) -> p k", k=KD)).then_inc(lnc_loaded, 16)
            for m, v in enumerate((ln0_g, ln0_b)):
                eng.dma_start(gb2[:, m, :], v.rearrange("(o n) -> o n", o=1).to_broadcast([P, D])).then_inc(gb0_loaded, 16)

            eng.drain().then_inc(y_evac, 1)
            eng.wait_ge(sp_in, 1)
            eng.activation(sp[:, 1, :], sp[:, 1, :], ACT.Exp).then_inc(sp_exp, 1)

            def norm_T(n, which, base):
                eng.wait_ge(var_ready, base + 1)
                eng.activation(rstd[:, :, 0], rstd[:, :, 1], ACT.Sqrt).then_inc(std_ready, 1)
                for c in range(0, 8, 2):
                    eng.wait_ge(xnT_done, base * 8 + c + 1)
                    for k in (2 * c, 2 * c + 1):
                        last = eng.activation(hT[:, k, :], ps[:, c, (k % 2) * T:(k % 2) * T + T], ACT.Identity,
                                              bias=lnc[:, which, 1, k:k + 1], scale=lnc[:, which, 0, k:k + 1])
                    last.then_inc(hT_act, 1)

            eng.wait_ge(lnc_loaded, 16 * 2 * (1 + 2 * L))
            norm_T(0, 0, 0)

            with eng.Fori(0, L) as l:
                eng.wait_ge(h_ready, (2 * l + 1) * NT)
                for m in range(1):
                    rb = att_rel_bias[bass.ds(l, 1)]
                    src = bass.AP(tensor=rb.tensor, offset=rb.offset + P + 1,
                                  ap=[[1, P], [att_rel_bias.shape[2], HEADS], [1, T]])
                    eng.dma_start(blocks(a_H, HEADS), src).then_inc(small_loaded.sem, 16)
                eng.dma_start(c_wa2, gla_wa2[bass.ds(l, 1)].rearrange("o r c -> (o r) c")).then_inc(small_loaded.sem, 16)
                eng.dma_start(c_wca, w_in[bass.ds(l, 1), :, C_A:C_A + RANK].rearrange("o (p k) n -> p (o k) n", k=KD)
                              ).then_inc(small_loaded.sem, 16)

                dest = {"dq": a_qT, "dk": a_kT, "dv": a_v, "cqk": c_qk, "cv": c_v, "cg": c_g, "ax": r_x, "ag": r_g,
                        "bc": b_c, "bh": b_h}

                def evacuate(s, func=ACT.Copy, scale=1.0):
                    d = dest[W_IN[s][0]]
                    for i in range(2):
                        eng.wait_ge(acc_full.sem, acc_full.at(l, 2 * s + i + 1))
                        eng.activation(d[:, i * 512:i * 512 + 512], ps[:, i, :], func, scale=scale
                                       ).then_inc(z_evac.sem, 1)

                evacuate(0, scale=float(P) ** -0.5)
                evacuate(1)
                evacuate(2)
                evacuate(3)
                eng.wait_ge(att_max.sem, att_max.at(l, 1))
                for hd in range(HEADS):
                    eng.activation(a_P[:, hd, 0:P], ps[:, 2 + hd, 0:P], ACT.Exp, bias=nmax[:, 0, hd:hd + 1],
                                   accum_out=rsum[:, 0, hd:hd + 1])
                    last = eng.activation(a_P[:, hd, P:384], ps[:, 2 + hd, P:384], ACT.Exp, bias=nmax[:, 1, hd:hd + 1],
                                          accum_out=rsum[:, 1, hd:hd + 1])
                last.then_inc(att_exp.sem, 1)
                evacuate(4)
                eng.wait_ge(att_pT.sem, att_pT.at(l, 1))
                eng.activation(a_PT, ps[:, 2:6, 0:384], ACT.Copy).then_inc(att_pTs.sem, 1)
                eng.wait_ge(ca_done.sem, ca_done.at(l, 1))
                eng.activation(c_aT, ps[0:RANK, 6, 0:T], ACT.Copy).then_inc(ca_evac.sem, 1)
                evacuate(5, ACT.Silu)
                eng.wait_ge(att_o.sem, att_o.at(l, 1))
                eng.activation(mixT[:, 12:16, :].rearrange("p k t -> p (k t)"), banks(6, 2), ACT.Copy
                               ).then_inc(att_done.sem, 1)
                eng.wait_ge(la_abs.sem, la_abs.at(l, 1))
                eng.activation(c_t1, c_t1, ACT.Exp)
                eng.drain()
                eng.activation(c_t1, c_t1, ACT.Ln, bias=1.0).then_inc(la_ln.sem, 1)
                eng.wait_ge(bc_ready.sem, bc_ready.at(l, 1))
                eng.activation(c_qd, c_bcum, ACT.Exp, scale=1.0 / TAU)
                eng.activation(c_ki, c_bcum, ACT.Exp, scale=-1.0 / TAU)
                eng.activation(c_ke, c_t1, ACT.Exp, scale=1.0 / TAU)
                eng.activation(blast[:], c_bcum.rearrange("p (n c) -> p n c", c=CH)[:, :, CH - 1], ACT.Exp,
                               scale=1.0 / TAU).then_inc(exps_ready.sem, 1)
                evacuate(6)
                eng.wait_ge(ke_T.sem, ke_T.at(l, 1))
                eng.activation(c_keT.rearrange("p t c -> p (t c)"), ps[:, 3, :], ACT.Copy).then_inc(ke_evac.sem, 1)
                evacuate(7, ACT.Gelu_apprx_tanh)
                eng.wait_ge(go_done.sem, go_done.at(l, 1))
                eng.activation(c_sq, banks(4, 2), ACT.Square).then_inc(sq_ready.sem, 1)
                for m, w in enumerate((lru_wa, lru_wx)):
                    eng.dma_start(r_w[:, m, :, :], w[bass.ds(l, 1)].rearrange("o h i j -> i (o h) j")
                                  ).then_inc(lru_loaded.sem, 16)
                eng.wait_ge(ms_done.sem, ms_done.at(l, 1))
                eng.activation(c_rs, banks(2, 2), ACT.Identity, bias=RMS_EPS, scale=1.0 / P)
                eng.drain()
                eng.activation(c_rs, c_rs, ACT.Sqrt).then_inc(ms_sqrt.sem, 1)
                evacuate(8)
                eng.wait_ge(gla_done.sem, gla_done.at(l, 1))
                eng.wait_ge(cur_ready, l + 1)
                eng.wait_ge(gates_done.sem, gates_done.at(l, 1))
                for m, (dst, name) in enumerate(((r_r, "lru_ba"), (r_i, "lru_bx"))):
                    for b in range(4):
                        col = ROWS[name][0] + b
                        last = eng.activation(dst[:, b * T:b * T + T], banks(2 + 4 * m, 2)[:, b * T:b * T + T],
                                              ACT.Sigmoid, bias=cur[:, col:col + 1])
                last.then_inc(gates_free.sem, 1)
                eng.drain()
                for b in range(4):
                    eng.activation(r_t[:, b * T:b * T + T], r_r[:, b * T:b * T + T], ACT.Tanh,
                                   scale=cur_cs[:, 0, b:b + 1])
                eng.drain()
                for b in range(4):
                    last = eng.activation(r_r[:, b * T:b * T + T], r_r[:, b * T:b * T + T], ACT.Exp,
                                          scale=cur_cs[:, 1, b:b + 1])
                last.then_inc(at_ready.sem, 1)
                evacuate(9)
                eng.wait_ge(om_ready.sem, om_ready.at(l, 1))
                eng.activation(r_t, r_t, ACT.Sqrt).then_inc(mult_ready.sem, 1)
                eng.wait_ge(mixb_ready.sem, mixb_ready.at(l, 2))
                eng.wait_ge(lru_done.sem, lru_done.at(l, 1))
                for m, v in enumerate((ln1_g, ln1_b)):
                    eng.dma_start(gb1[:, m, :], v[bass.ds(l, 1)].to_broadcast([P, D])).then_inc(gb1_loaded.sem, 16)
                eng.dma_start(wr[:, :, 0:G], w_rg[bass.ds(l, 1)].rearrange("o (p k) g -> p (o k) g", k=KD)
                              ).then_inc(router_loaded.sem, 16)
                eng.dma_start(wr[:, :, G:NR], w_re[bass.ds(l, 1)].rearrange("o (p k) g -> p (o k) g", k=KD)
                              ).then_inc(router_loaded.sem, 16)
                eng.dma_start(br[:, 0:G], b_rg[bass.ds(l, 1)].to_broadcast([P, G])).then_inc(router_loaded.sem, 16)
                eng.dma_start(br[:, G:NR], b_re[bass.ds(l, 1)].to_broadcast([P, E])).then_inc(router_loaded.sem, 16)

                norm_T_dyn(eng, l, 0)
                eng.wait_ge(ex_in.sem, ex_in.at(l, 1))
                eng.activation(ex, ex, ACT.Exp).then_inc(ex_ready.sem, 1)
                for k in range(0, KD, 2):
                    eng.wait_ge(gath_done.sem, gath_done.at(l, k + 1))
                    eng.activation(xgT[:, k, 0:S], ps[:, k % 8, :], ACT.Identity,
                                   bias=cur_ln[:, 0, 1, k:k + 1], scale=cur_ln[:, 0, 0, k:k + 1]
                                   ).then_inc(gath_act.sem, 1)
                eng.wait_ge(pwT_done.sem, pwT_done.at(l, 1))
                eng.wait_ge(h_ready, (2 * l + 2) * NT)
                eng.activation(pw.rearrange("p b t -> p (b t)"), banks(6, 2), ACT.Copy).then_inc(pw_ready.sem, 1)
                with eng.Fori(0, E) as e:
                    first, n, g0 = expert_row(eng, 0, e), expert_row(eng, 1, e), expert_row(eng, 2, e)
                    with eng.Fori(0, n) as j:
                        eng.wait_ge(gu_done, g0 + j + 2)
                        eng.activation(sgate, ps[:, 0, 0:256], ACT.Silu).then_inc(sg_ready, 1)
                        eng.wait_ge(hmT_done, g0 + j + 1)
                        eng.activation(hmT.rearrange("p q n -> p (q n)"), ps[:, 1, 0:256], ACT.Copy
                                       ).then_inc(hmT_ready, 1)
                        eng.wait_ge(y_done, g0 + j + 1)
                        eng.activation(yraw, banks(2, 2), ACT.Copy).then_inc(yraw_ready, 1)
                        eng.wait_ge(yt_done, g0 + j + 1)
                        dst = yT.rearrange("p (i c q) s -> p c i q s", i=2, c=2)
                        src = banks(4, 2).rearrange("p (i q c s) -> p c i q s", i=2, q=4, c=2)
                        for c in range(2):
                            last = eng.activation(dst[:, c, :, :, bass.ds(block_start(first, j), BLK)], src[:, c], ACT.Copy)
                        last.then_inc(y_evac, 1)
                for c in range(0, 16, 2):
                    eng.wait_ge(yS_done.sem, yS_done.at(l, c + 1))
                    eng.activation(ySort[:, c // 4, (c % 4) * 512:(c % 4) * 512 + 512], ps[:, c % 8, :], ACT.Copy
                                   ).then_inc(yS_act.sem, 1)
                eng.wait_ge(yS_done.sem, yS_done.at(l, 16))
                for m, v in enumerate((ln2_g, ln2_b)):
                    eng.dma_start(gb2[:, m, :], v[bass.ds(l, 1)].to_broadcast([P, D])).then_inc(gb2_loaded.sem, 16)
                norm_T_dyn(eng, l, 1)

        @block.tensor
        def _(eng):
            def turn(n):
                eng.wait_ge(xn_ready, (n + 1) * NT)
                for c in range(8):
                    for k in (2 * c, 2 * c + 1):
                        for t in range(NT):
                            o = (k % 2) * T + t * P
                            last = eng.transpose(ps[:, c, o:o + P], h[:, t, k:D:KD], ident[:])
                    last.then_inc(xnT_done, 1)

            eng.wait_ge(consts, 1)
            eng.wait_ge(par_loaded, 16 * 8 * L)
            eng.transpose(ps[:, 0, 0:L * NROWS], par_rows[0:L * NROWS, :], ident[0:L * NROWS, 0:L * NROWS]
                          ).then_inc(par_T, 1)
            eng.wait_ge(par_ready, 1)
            turn(0)
            eng.drain().then_inc(half_used, HALVES)
            eng.drain().then_inc(gu_done, 1)

            def project(l, s, token_major):
                slot = s % SLOTS
                w = slab(slot)
                n_load = l * PER_SLOT + s // SLOTS + 1
                eng.wait_ge(slab_loaded[slot][0], 16 * n_load)
                eng.wait_ge(slab_loaded[slot][1], 16 * n_load)
                for i in range(2):
                    if s >= 1:
                        eng.wait_ge(z_evac.sem, z_evac.at(l, 2 * (s - 1) + i + 1))
                    if token_major:
                        for k in range(KD):
                            last = eng.matmul(ps[:, i, :], hT[:, k, i * P:i * P + P], w[:, k, :],
                                              start=(k == 0), stop=(k == KD - 1))
                    else:
                        for b in (2 * i, 2 * i + 1):
                            for k in range(KD):
                                last = eng.matmul(ps[:, i, (b % 2) * T:(b % 2) * T + T], w[:, k, b * P:b * P + P],
                                                  hT[:, k, :], start=(k == 0), stop=(k == KD - 1))
                    last.then_inc(acc_full.sem, 1)
                return last

            def release():
                eng.drain().then_inc(half_used, 2)

            with eng.Fori(0, L) as l:
                eng.wait_ge(hT_act, (2 * l + 1) * 4)
                eng.wait_ge(hT_dve, (2 * l + 1) * 4)
                for s in range(4):
                    project(l, s, W_IN[s][0] == "dv")
                    release()
                eng.wait_ge(z_evac.sem, z_evac.at(l, 4))
                eng.wait_ge(small_loaded.sem, small_loaded.at(l, 48))
                qT, kT, band = blocks(a_qT, 4), blocks(a_kT, 4), blocks(a_H, 4)
                for hd in range(HEADS):
                    for t in range(NT):
                        for sbk in range(t + 1):
                            o = ps[:, 2 + hd, (t + sbk) * P:(t + sbk) * P + P]
                            eng.matmul(o, qT[:, hd, t * P:t * P + P], kT[:, hd, sbk * P:sbk * P + P], start=True, stop=False)
                            last = eng.matmul(o, band[:, hd, (t - sbk) * P:(t - sbk) * P + P], anti[:],
                                              start=False, stop=(sbk < t))
                            if sbk == t:
                                last = eng.matmul(o, lo_row[:], hi_row[:], start=False, stop=True)
                last.then_inc(att_scores.sem, 1)
                project(l, 4, True)
                release()
                eng.wait_ge(att_prob.sem, att_prob.at(l, 1))
                for hd in range(HEADS):
                    for c in range(3):
                        last = eng.transpose(ps[:, 2 + hd, c * P:c * P + P], a_P[:, hd, c * P:c * P + P], ident[:])
                last.then_inc(att_pT.sem, 1)
                for k in range(KD):
                    last = eng.matmul(ps[0:RANK, 6, 0:T], c_wca[:, k, :], hT[:, k, :], start=(k == 0), stop=(k == KD - 1))
                last.then_inc(ca_done.sem, 1)
                project(l, 5, False)
                release()
                eng.wait_ge(att_pTs.sem, att_pTs.at(l, 1))
                eng.wait_ge(ca_evac.sem, ca_evac.at(l, 1))
                eng.wait_ge(z_evac.sem, z_evac.at(l, 6))
                v = blocks(a_v, NT)
                for hd in range(HEADS):
                    o = ps[:, 6 + hd // 2, (hd % 2) * T:(hd % 2) * T + T]
                    eng.matmul(o, v[:, 0, hd * P:hd * P + P], a_PT[:, hd, 0:T], start=True, stop=False)
                    last = eng.matmul(o[:, P:T], v[:, 1, hd * P:hd * P + P], a_PT[:, hd, T:384], start=False, stop=True)
                last.then_inc(att_o.sem, 1)
                for b in range(2):
                    last = eng.matmul(ps[:, 2, b * T:b * T + T], c_wa2[:, b * P:b * P + P], c_aT, start=True, stop=True)
                last.then_inc(la_done.sem, 1)
                project(l, 6, False)
                release()
                eng.wait_ge(qk_ready.sem, qk_ready.at(l, 1))
                for b in range(2):
                    for t in range(NT):
                        last = eng.transpose(ps[:, 3, t * 256 + b * P:t * 256 + b * P + P],
                                             c_ke[:, b * T + t * P:b * T + t * P + P], ident[:])
                last.then_inc(ke_T.sem, 1)
                for par_ in range(2):
                    for b in range(2):
                        r0 = par_ * 64
                        for t in range(NT):
                            c0 = b * T + t * P
                            last = eng.matmul(ps[:, 4 + par_, (b * NT + t) * P:(b * NT + t) * P + P],
                                              c_ki[r0:r0 + 64, c0:c0 + P], c_qd[r0:r0 + 64, c0:c0 + P],
                                              start=True, stop=True)
                last.then_inc(gsc_done.sem, 1)
                project(l, 7, False)
                release()
                eng.wait_ge(ke_evac.sem, ke_evac.at(l, 1))
                eng.wait_ge(att_done.sem, att_done.at(l, 1))
                vv = blocks(c_v, NT)
                for n in range(3):
                    r0 = (n % 2) * CH
                    for b in range(2):
                        last = eng.matmul(ps[:, (6, 7, 2)[n], b * 256:b * 256 + 256],
                                          c_keT[r0:r0 + CH, n // 2, b * P:b * P + P],
                                          vv[r0:r0 + CH, n // 2, b * 256:b * 256 + 256], start=True, stop=True)
                last.then_inc(kv_done.sem, 1)
                eng.wait_ge(gsc_evac.sem, gsc_evac.at(l, 1))
                eng.wait_ge(state_ready.sem, state_ready.at(l, 1))
                for hd in range(HEADS):
                    b, r0 = hd // 2, (hd % 2) * 64
                    for t in range(NT):
                        c0 = b * T + t * P
                        eng.matmul(ps[:, 4 + hd % 2, c0:c0 + P], vv[:, t, hd * P:hd * P + P],
                                   c_scT[:, (hd % 2) * 4 + b * NT + t, :], start=True, stop=False)
                        for n in (2 * t, 2 * t + 1):
                            if n:
                                o0 = b * T + n * CH
                                last = eng.matmul(ps[:, 4 + hd % 2, o0:o0 + CH], c_state[r0:r0 + 64, n - 1, b, :],
                                                  c_qd[r0:r0 + 64, b * T + n * CH:b * T + n * CH + CH],
                                                  start=False, stop=(n % 2 == 1))
                last.then_inc(go_done.sem, 1)
                eng.wait_ge(sq_ready.sem, sq_ready.at(l, 1))
                for b in range(2):
                    last = eng.matmul(ps[:, 2 + b, :], ones[:], c_sq[:, b * 512:b * 512 + 512], start=True, stop=True)
                last.then_inc(ms_done.sem, 1)
                project(l, 8, False)
                release()
                eng.wait_ge(u_ready.sem, u_ready.at(l, 1))
                eng.wait_ge(lru_loaded.sem, lru_loaded.at(l, 32))
                eng.wait_ge(ms_sqrt.sem, ms_sqrt.at(l, 1))
                for m in range(2):
                    for b in range(4):
                        last = eng.matmul(banks(2 + 4 * m, 2)[:, b * T:b * T + T], r_w[:, m, b, :],
                                          r_u[:, b * T:b * T + T], start=True, stop=True)
                last.then_inc(gates_done.sem, 1)
                project(l, 9, False)
                release()
                project(l, 10, False)
                release()

                eng.wait_ge(att_done.sem, att_done.at(l, 1))
                eng.wait_ge(gla_done.sem, gla_done.at(l, 1))
                eng.wait_ge(lru_done.sem, lru_done.at(l, 1))
                order = [0, 1, 2, 3, 8, 9, 10, 11, 12, 13, 14, 15, 4, 5, 6, 7]
                for c in range(N_OUT):
                    s = N_IN + c
                    n_load = l * PER_SLOT + s // SLOTS + 1
                    eng.wait_ge(slab_loaded[s % SLOTS][0], 16 * n_load)
                    eng.wait_ge(slab_loaded[s % SLOTS][1], 16 * n_load)
                    for t in range(NT):
                        if c == 0:
                            eng.wait_ge(mixb_ready.sem, mixb_ready.at(l, 2))
                        else:
                            eng.wait_ge(res_add.sem, res_add.at(l, 2 * c - 1 + t))
                        for i, k in enumerate(order):
                            last = eng.matmul(ps[:, t, :], mixT[:, k, t * P:t * P + P], slab(s % SLOTS)[:, k, :],
                                              start=(i == 0), stop=(i == KD - 1))
                        last.then_inc(acc_full.sem, 1)
                    release()

                turn(2 * l + 1)
                eng.wait_ge(router_loaded.sem, router_loaded.at(l, 64))
                eng.wait_ge(hT_act, (2 * l + 2) * 4)
                eng.wait_ge(hT_dve, (2 * l + 2) * 4)
                for t in range(NT):
                    for k in range(KD):
                        last = eng.matmul(ps[:, 0, t * NR:t * NR + NR], hT[:, k, t * P:t * P + P], wr[:, k, :],
                                          start=(k == 0), stop=(k == KD - 1))
                last.then_inc(logits_done.sem, 1)
                eng.wait_ge(m_ready.sem, m_ready.at(l, 1))
                eng.matmul(ps[:, 1, 0:16], before[:], M[:, 2, 0, :], start=True, stop=True)
                eng.matmul(ps[:, 1, 16:32], ones[:], M[:, 2, 0, :], start=True, stop=False)
                eng.matmul(ps[:, 1, 16:32], before[:], M[:, 2, 1, :], start=False, stop=True)
                eng.matmul(ps[:, 1, 32:48], ones[:], M[:, 2, 0, :], start=True, stop=False)
                eng.matmul(ps[:, 1, 32:48], ones[:], M[:, 2, 1, :], start=False, stop=True).then_inc(ranks_done.sem, 1)
                eng.wait_ge(hot_ready.sem, hot_ready.at(l, 1))
                for k in range(KD):
                    if k >= 8:
                        if k % 2 == 0:
                            eng.wait_ge(gath_act.sem, gath_act.at(l, (k - 8) // 2 + 1))
                        else:
                            eng.wait_ge(gath_dve.sem, gath_dve.at(l, (k - 8) // 2 + 1))
                    for t in range(NT):
                        last = eng.matmul(ps[:, k % 8, :], h[:, t, k:D:KD], hot[:, t, :], start=(t == 0), stop=(t == NT - 1))
                    last.then_inc(gath_done.sem, 1)
                eng.wait_ge(gath_act.sem, gath_act.at(l, 8))
                eng.wait_ge(gath_dve.sem, gath_dve.at(l, 8))
                for sbk in range(4):
                    for t in range(NT):
                        last = eng.transpose(banks(6, 2)[:, sbk * T + t * P:sbk * T + t * P + P],
                                             hotw[:, t, sbk * P:sbk * P + P], ident[:])
                last.then_inc(pwT_done.sem, 1)

                def expert_block(g, e, last_block):
                    n_load = l * PER_SLOT + FIRST_E // SLOTS + e + 1
                    eng.wait_ge(xe_ready, g + 1)
                    for i in range(2):
                        eng.wait_ge(slab_loaded[0][i], 16 * n_load)
                        eng.wait_ge(slab_loaded[1][i], 16 * n_load)
                        for k in range(8 * i, 8 * i + 8):
                            for c in range(2):
                                last = eng.matmul(ps[64 * c:64 * c + BLK, 0, :], xe[:, k, :],
                                                  ring[:, 0:2, k * 512 + c * 256:k * 512 + c * 256 + 256],
                                                  start=(k == 0), stop=(k == KD - 1))
                        if i == 1:
                            last.then_inc(gu_done, 1)
                        if last_block:
                            release()
                    eng.wait_ge(hm_ready, g + 1)
                    for q in range(2):
                        last = eng.transpose(ps[:, 1, q * P:q * P + P], hmid[:, q * P:q * P + P], ident[:])
                    last.then_inc(hmT_done, 1)
                    eng.wait_ge(hmT_ready, g + 1)
                    for f in range(KF):
                        if f % 2 == 0:
                            eng.wait_ge(slab_loaded[2][f // 2], 16 * n_load)
                        for ch in range(4):
                            r0 = 64 * (ch % 2)
                            last = eng.matmul(ps[r0:r0 + BLK, 2 + ch // 2, :], hmT[:, f % 2, 64 * (f // 2):64 * (f // 2) + BLK],
                                              slab_down(2)[:, f, ch * 512:ch * 512 + 512],
                                              start=(f == 0), stop=(f == KF - 1))
                    last.then_inc(y_done, 1)
                    if last_block:
                        release()
                    eng.wait_ge(yraw_ready, g + 1)
                    eng.wait_ge(y_evac, g + 1)
                    for q in range(8):
                        last = eng.transpose(banks(4, 2)[:, q * P:q * P + P], yraw[:, q * P:q * P + P], ident[:])
                    last.then_inc(yt_done, 1)

                with eng.Fori(0, E) as e:
                    n, g0 = expert_row(eng, 1, e), expert_row(eng, 2, e)
                    with eng.If(n > 1):
                        with eng.Fori(0, n - 1) as j:
                            expert_block(g0 + j, e, False)
                    expert_block(g0 + n - 1, e, True)

                n, g0 = expert_row(eng, 1, E - 1), expert_row(eng, 2, E - 1)
                eng.wait_ge(y_evac, g0 + n + 1)
                for c in range(16):
                    if c >= 8:
                        if c % 2 == 0:
                            eng.wait_ge(yS_act.sem, yS_act.at(l, (c - 8) // 2 + 1))
                        else:
                            eng.wait_ge(yS_dve.sem, yS_dve.at(l, (c - 8) // 2 + 1))
                    for q in range(4):
                        last = eng.transpose(ps[:, c % 8, q * P:q * P + P],
                                             yT[:, (c % 4) * 4 + q, (c // 4) * P:(c // 4) * P + P], ident[:])
                    last.then_inc(yS_done.sem, 1)
                eng.wait_ge(yS_act.sem, yS_act.at(l, 8))
                eng.wait_ge(yS_dve.sem, yS_dve.at(l, 8))
                eng.wait_ge(pw_ready.sem, pw_ready.at(l, 1))
                for c in range(N_OUT):
                    for t in range(NT):
                        for sbk in range(4):
                            last = eng.matmul(ps[:, 2 * c + t, :], pw[:, sbk, t * P:t * P + P],
                                              ySort[:, sbk, c * 512:c * 512 + 512], start=(sbk == 0), stop=(sbk == 3))
                        last.then_inc(sc_done.sem, 1)
                turn(2 * l + 2)

        @block.vector
        def _(eng):
            def tt(o, a, b, op):
                return eng.tensor_tensor(o, a, b, op)

            def ts(o, a, s1, s2, op0, op1=None):
                return eng.tensor_scalar(o, a, s1, s2, op0, op1) if op1 is not None else eng.tensor_scalar(o, a, s1, None, op0)

            def norm(n, gb):
                for t in range(NT):
                    for c in range(4):
                        eng.bn_stats(stats[:, t, c, :], h[:, t, c * 512:c * 512 + 512])
                eng.drain()
                for t in range(NT):
                    eng.bn_aggr(mv[:, t, :], stats[:, t, :, :].rearrange("p c s -> p (c s)"))
                eng.drain()
                ts(rstd[:, :, 1], mv[:, :, 1], LN_EPS, None, ALU.add).then_inc(var_ready, 1)
                eng.wait_ge(std_ready, n + 1)
                eng.reciprocal(rstd[:, :, 1], rstd[:, :, 0])
                eng.drain()
                for t in range(NT):
                    ts(h[:, t, :], h[:, t, :], mv[:, t, 0:1], rstd[:, t, 1:2], ALU.subtract, ALU.mult).then_inc(xn_ready, 1)
                for c in range(1, 8, 2):
                    eng.wait_ge(xnT_done, n * 8 + c + 1)
                    for k in (2 * c, 2 * c + 1):
                        g_, b_ = gb[:, 0, k:k + 1], gb[:, 1, k:k + 1]
                        last = ts(hT[:, k, :], ps[:, c, (k % 2) * T:(k % 2) * T + T], g_, b_, ALU.mult, ALU.add)
                    last.then_inc(hT_dve, 1)

            def column(l, name, i):
                return cur[:, ROWS[name][0] + i:ROWS[name][0] + i + 1]

            eng.wait_ge(par_T, 1)
            eng.tensor_copy(par[:].rearrange("p l r -> p (l r)"), ps[:, 0, 0:L * NROWS]).then_inc(par_ready, 1)
            eng.drain()
            lam = par[:, :, ROWS["lru_lam"][0]:ROWS["lru_lam"][0] + 4]
            s0, s1, s2, s3 = (sp[:, i, :].rearrange("p (l b) -> p l b", l=L) for i in range(4))
            ts(s0, lam, -1.0, 0.0, ALU.mult, ALU.max)
            eng.scalar_tensor_tensor(s1, lam, -1.0, lam, ALU.mult, ALU.min).then_inc(sp_in, 1)
            eng.wait_ge(sp_exp, 1)
            ts(s2, s1, 2.0, None, ALU.add)
            eng.drain()
            eng.reciprocal(s2, s2)
            eng.drain()
            tt(s1, s1, s2, ALU.mult)
            eng.drain()
            tt(s2, s1, s1, ALU.mult)
            eng.drain()
            ts(s3, s2, 1.0 / 17.0, 1.0 / 15.0, ALU.mult, ALU.add)
            for d in (13.0, 11.0, 9.0, 7.0, 5.0, 3.0, 1.0):
                eng.drain()
                tt(s3, s3, s2, ALU.mult)
                eng.drain()
                ts(s3, s3, 1.0 / d, None, ALU.add)
            eng.drain()
            tt(s3, s3, s1, ALU.mult)
            eng.drain()
            eng.scalar_tensor_tensor(s3, s3, 2.0, s0, ALU.mult, ALU.add)
            eng.drain()
            ts(cs[:], s3, LRU_C, None, ALU.mult)
            ts(csn[:], s3, -LRU_C, None, ALU.mult).then_inc(cs_ready, 1)

            eng.wait_ge(x_loaded, 16)
            eng.wait_ge(lnc_loaded, 16 * 2 * (1 + 2 * L))
            norm(0, lnc[:, 0])

            with eng.Fori(0, L) as l:
                eng.wait_ge(hT_act, (2 * l + 1) * 4)
                eng.tensor_copy(cur[:], par[:, bass.ds(l, 1), :].rearrange("p o r -> p (o r)"))
                eng.tensor_copy(cur_cs[:, 0, :], cs[:, bass.ds(l, 1), :].rearrange("p o r -> p (o r)"))
                eng.tensor_copy(cur_cs[:, 1, :], csn[:, bass.ds(l, 1), :].rearrange("p o r -> p (o r)"))
                eng.tensor_copy(cur_ln[:], lnc[:, bass.ds(2 * l + 1, 2), :, :]).then_inc(cur_ready, 1)
                eng.wait_ge(att_scores.sem, att_scores.at(l, 1))
                eng.tensor_reduce(nmax[:, 0, :], ps[:, 2:6, 0:P], AX.X, ALU.max, negate=True)
                eng.tensor_reduce(nmax[:, 1, :], ps[:, 2:6, P:384], AX.X, ALU.max, negate=True).then_inc(att_max.sem, 1)
                eng.wait_ge(att_exp.sem, att_exp.at(l, 1))
                eng.reciprocal(rsum[:], rsum[:])
                eng.drain()
                for hd in range(HEADS):
                    ts(a_P[:, hd, 0:P], a_P[:, hd, 0:P], rsum[:, 0, hd:hd + 1], None, ALU.mult)
                    last = ts(a_P[:, hd, P:384], a_P[:, hd, P:384], rsum[:, 1, hd:hd + 1], None, ALU.mult)
                last.then_inc(att_prob.sem, 1)

                eng.wait_ge(la_done.sem, la_done.at(l, 1))
                for b in range(2):
                    ts(c_bcum[:, b * T:b * T + T], ps[:, 2, b * T:b * T + T], column(l, "gla_ba2", b), None, ALU.add)
                eng.drain()
                eng.scalar_tensor_tensor(c_t1, c_bcum, -1.0, c_bcum, ALU.mult, ALU.min).then_inc(la_abs.sem, 1)
                eng.wait_ge(la_ln.sem, la_ln.at(l, 1))
                eng.scalar_tensor_tensor(c_t1, c_bcum, 0.0, c_t1, ALU.min, ALU.subtract)
                eng.drain()
                for i in range(8):
                    sl = slice(i * CH, i * CH + CH)
                    eng.tensor_tensor_scan(c_bcum[:, sl], c_t1[:, sl], c_t1[:, sl], 0.0, ALU.add, ALU.bypass)
                eng.drain()
                bc3 = c_bcum.rearrange("p (n c) -> p n c", c=CH)
                tt(c_t1.rearrange("p (n c) -> p n c", c=CH), bc3[:, :, CH - 1:CH].to_broadcast([P, 8, CH]), bc3,
                   ALU.subtract).then_inc(bc_ready.sem, 1)
                eng.wait_ge(exps_ready.sem, exps_ready.at(l, 1))
                eng.scalar_tensor_tensor(c_qd, c_qk[:, 0:512], 0.125, c_qd, ALU.mult, ALU.mult)
                tt(c_ki, c_ki, c_qk[:, 512:1024], ALU.mult)
                tt(c_ke, c_ke, c_qk[:, 512:1024], ALU.mult).then_inc(qk_ready.sem, 1)
                eng.drain()
                eng.wait_ge(z_evac.sem, z_evac.at(l, 14))
                u, xin = blocks(r_u, 4), blocks(r_x, 4)
                for b in range(4):
                    ts(u[:, b, :], xin[:, b, :], column(l, "conv_a_w", 12 + b), column(l, "conv_a_b", b), ALU.mult, ALU.add)
                for d in range(1, 4):
                    eng.drain()
                    for b in range(4):
                        last = eng.scalar_tensor_tensor(u[:, b, d:T], xin[:, b, 0:T - d],
                                                        column(l, "conv_a_w", (3 - d) * 4 + b), u[:, b, d:T],
                                                        ALU.mult, ALU.add)
                last.then_inc(u_ready.sem, 1)
                eng.wait_ge(gsc_done.sem, gsc_done.at(l, 1))
                eng.memset(c_scT, 0.0)
                eng.drain()
                mask = causal[:].bitcast(U32).rearrange("p (o t) -> p o t", o=1).to_broadcast([P, 4, P])
                for i in range(2):
                    last = eng.copy_predicated(c_scT[:, 4 * i:4 * i + 4, :], mask,
                                               ps[:, 4 + i, :].rearrange("p (j t) -> p j t", j=4))
                last.then_inc(gsc_evac.sem, 1)
                eng.wait_ge(kv_done.sem, kv_done.at(l, 1))
                for n in range(3):
                    bank = (6, 7, 2)[n]
                    for b in range(2):
                        for i in range(2):
                            r = slice(64 * i, 64 * i + 64)
                            src = ps[r, bank, b * 256 + i * P:b * 256 + i * P + P]
                            if n == 0:
                                last = eng.tensor_copy(c_state[r, 0, b, :], src)
                            else:
                                last = eng.scalar_tensor_tensor(c_state[r, n, b, :], c_state[r, n - 1, b, :],
                                                                blast[r, b * 4 + n:b * 4 + n + 1], src, ALU.mult, ALU.add)
                    if n < 2:
                        eng.drain()
                last.then_inc(state_ready.sem, 1)
                eng.wait_ge(ms_sqrt.sem, ms_sqrt.at(l, 1))
                eng.reciprocal(c_rs, c_rs)
                eng.drain()
                tt(c_rs, c_rs, banks(4, 2), ALU.mult)
                eng.drain()
                for b in range(4):
                    last = eng.scalar_tensor_tensor(mixT[:, 8 + b, :], c_rs[:, bank_order(b) * T:bank_order(b) * T + T],
                                                    column(l, "gla_norm_w", b),
                                                    c_g[:, b * T:b * T + T], ALU.mult, ALU.mult)
                last.then_inc(gla_done.sem, 1)

                eng.wait_ge(at_ready.sem, at_ready.at(l, 1))
                tt(r_i, r_i, r_u, ALU.mult)
                ts(r_x, r_t, 1.0, None, ALU.add)
                eng.drain()
                eng.reciprocal(r_x, r_x)
                eng.drain()
                eng.scalar_tensor_tensor(r_t, r_t, 2.0, r_x, ALU.mult, ALU.mult).then_inc(om_ready.sem, 1)
                eng.wait_ge(z_evac.sem, z_evac.at(l, 20))
                tt(b_p, b_c, b_h, ALU.mult)
                eng.drain()
                cv, pp = blocks(b_cv, 4), blocks(b_p, 4)
                for b in range(4):
                    ts(cv[:, b, :], pp[:, b, :], column(l, "conv_b_w", 8 + b), None, ALU.mult)
                for d in range(1, 3):
                    eng.drain()
                    for b in range(4):
                        eng.scalar_tensor_tensor(cv[:, b, d:T], pp[:, b, 0:T - d], column(l, "conv_b_w", (2 - d) * 4 + b),
                                                 cv[:, b, d:T], ALU.mult, ALU.add)
                eng.wait_ge(mult_ready.sem, mult_ready.at(l, 1))
                tt(r_i, r_i, r_t, ALU.mult)
                eng.drain()
                for b in range(4):
                    sl = slice(b * T, b * T + T)
                    eng.tensor_tensor_scan(r_u[:, sl], r_r[:, sl], r_i[:, sl], 0.0, ALU.mult, ALU.add)
                eng.drain()
                tt(mixT[:, 0:4, :].rearrange("p k t -> p (k t)"), r_u, r_g, ALU.mult).then_inc(lru_done.sem, 1)
                for i in range(2):
                    eng.wait_ge(acc_full.sem, acc_full.at(l, 21 + i))
                    tt(mixT[:, 4 + 2 * i:6 + 2 * i, :].rearrange("p k t -> p (k t)"), b_cv[:, i * 512:i * 512 + 512],
                       ps[:, i, :], ALU.mult).then_inc(mixb_ready.sem, 1)

                eng.wait_ge(h_ready, (2 * l + 1) * NT)
                for c in range(N_OUT):
                    for t in range(NT):
                        eng.wait_ge(acc_full.sem, acc_full.at(l, 2 * (N_IN + c) + t + 1))
                        sl = h[:, t, c * 512:c * 512 + 512]
                        eng.scalar_tensor_tensor(sl, sl, ALPHA, ps[:, t, :], ALU.mult, ALU.add).then_inc(res_add.sem, 1)
                eng.drain()
                norm(2 * l + 1, cur_ln[:, 0])

                eng.wait_ge(router_loaded.sem, router_loaded.at(l, 64))
                eng.wait_ge(logits_done.sem, logits_done.at(l, 1))
                tt(lg, ps[:, 0, 0:NT * NR].rearrange("p (t n) -> p t n", t=NT),
                   br.rearrange("p (o n) -> p o n", o=1).to_broadcast([P, NT, NR]), ALU.add)
                eng.drain()

                def first_of(dst, vals, top):
                    eng.tensor_reduce(top, vals, AX.X, ALU.max)
                    eng.drain()
                    tt(rk, vals, top.to_broadcast([P, NT, 4]), ALU.is_equal)
                    eng.drain()
                    tt(rk, rk, desc[:].rearrange("p (o n) -> p o n", o=1).to_broadcast([P, NT, 4]), ALU.mult)
                    eng.drain()
                    eng.tensor_reduce(rkm, rk, AX.X, ALU.max)
                    eng.drain()
                    tt(dst, rk, rkm.to_broadcast([P, NT, 4]), ALU.is_equal)
                    eng.drain()

                first_of(goh, lg[:, :, 0:G], gmax)
                tt(ex[:, :, 0:4], lg[:, :, 0:G], gmax.to_broadcast([P, NT, 4]), ALU.subtract)
                for g in range(G):
                    tt(t16[:, :, 4 * g:4 * g + 4], lg[:, :, G + 4 * g:G + 4 * g + 4],
                       goh[:, :, g:g + 1].to_broadcast([P, NT, 4]), ALU.mult)
                eng.drain()
                eng.tensor_reduce(eg, t16.rearrange("p t (g e) -> p t e g", g=4), AX.X, ALU.add)
                eng.drain()
                first_of(oh[:, 0], eg, emax[:, 0])
                eng.scalar_tensor_tensor(eg, oh[:, 0], -BIG, eg, ALU.mult, ALU.add)
                eng.drain()
                first_of(oh[:, 1], eg, emax[:, 1])
                tt(ex[:, :, 4:5], emax[:, 1], emax[:, 0], ALU.subtract).then_inc(ex_in.sem, 1)
                for i in range(2):
                    for g in range(G):
                        tt(M[:, i, :, 4 * g:4 * g + 4], oh[:, i], goh[:, :, g:g + 1].to_broadcast([P, NT, 4]), ALU.mult)
                eng.drain()
                tt(M[:, 2], M[:, 0], M[:, 1], ALU.add).then_inc(m_ready.sem, 1)
                eng.wait_ge(ex_ready.sem, ex_ready.at(l, 1))
                eng.tensor_reduce(gval, ex[:, :, 0:4], AX.X, ALU.add)
                ts(wts[:, 1], ex[:, :, 4:5], 1.0, None, ALU.add)
                eng.drain()
                tt(gval, gval, wts[:, 1], ALU.mult)
                eng.drain()
                eng.reciprocal(wts[:, 0], gval)
                eng.drain()
                tt(wts[:, 1], wts[:, 0], ex[:, :, 4:5], ALU.mult)
                eng.wait_ge(ranks_done.sem, ranks_done.at(l, 1))
                eng.tensor_copy(tab[:, 0, :], ps[:, 1, 32:48])
                eng.drain()
                ts(tab[:, 1, :], tab[:, 0, :], float(BLK), 1.0, ALU.is_gt, ALU.add)
                for lim in range(2 * BLK, T, BLK):
                    eng.drain()
                    eng.scalar_tensor_tensor(tab[:, 1, :], tab[:, 0, :], float(lim), tab[:, 1, :], ALU.is_gt, ALU.add)
                eng.drain()
                for i in range(2):
                    eng.tensor_tensor_scan(scn[:, i, :], tab[:, i, :], tab[:, i, :], 0.0 if i == 0 else carry[:],
                                           ALU.add, ALU.bypass)
                eng.drain()
                tt(tab[:, 0, :], scn[:, 0, :], tab[:, 0, :], ALU.subtract)
                tt(tab[:, 2, :], scn[:, 1, :], tab[:, 1, :], ALU.subtract)
                eng.tensor_copy(carry[:], scn[:, 1, 15:16])
                eng.drain()
                eng.tensor_copy(tabi[:, 0:3, :], tab).then_inc(tab_ready.sem, 1)
                for t in range(NT):
                    tt(pos[:, t, :], ps[:, 1, 16 * t:16 * t + 16], tab[:, 0, :], ALU.add)
                eng.drain()
                for i in range(2):
                    tt(t16, M[:, i], pos, ALU.mult)
                    eng.drain()
                    eng.tensor_reduce(pos12[:, i], t16, AX.X, ALU.add)
                    eng.drain()
                for t in range(NT):
                    ts(hot[:, t, :], slot_iota[:], pos12[:, 0, t, :], None, ALU.is_equal)
                eng.drain()
                for t in range(NT):
                    last = eng.scalar_tensor_tensor(hot[:, t, :], slot_iota[:], pos12[:, 1, t, :], hot[:, t, :],
                                                    ALU.is_equal, ALU.add)
                last.then_inc(hot_ready.sem, 1)
                eng.memset(xgT[:, :, S:SP_], 0.0)
                ht = area(46, 512)
                for t in range(NT):
                    ts(hotw[:, t, :], slot_iota[:], pos12[:, 0, t, :], wts[:, 0, t, :], ALU.is_equal, ALU.mult)
                    ts(ht, slot_iota[:], pos12[:, 1, t, :], wts[:, 1, t, :], ALU.is_equal, ALU.mult)
                    eng.drain()
                    tt(hotw[:, t, :], hotw[:, t, :], ht, ALU.add)
                    eng.drain()
                for k in range(1, KD, 2):
                    eng.wait_ge(gath_done.sem, gath_done.at(l, k + 1))
                    ts(xgT[:, k, 0:S], ps[:, k % 8, :], cur_ln[:, 0, 0, k:k + 1],
                       cur_ln[:, 0, 1, k:k + 1], ALU.mult, ALU.add).then_inc(gath_dve.sem, 1)

                with eng.Fori(0, E) as e:
                    n, g0 = expert_row(eng, 1, e), expert_row(eng, 2, e)
                    with eng.Fori(0, n) as j:
                        eng.wait_ge(sg_ready, g0 + j + 1)
                        tt(hmid, sgate, ps[:, 0, 256:512], ALU.mult).then_inc(hm_ready, 1)

                for c in range(1, 16, 2):
                    eng.wait_ge(yS_done.sem, yS_done.at(l, c + 1))
                    eng.tensor_copy(ySort[:, c // 4, (c % 4) * 512:(c % 4) * 512 + 512], ps[:, c % 8, :]
                                    ).then_inc(yS_dve.sem, 1)
                eng.wait_ge(h_ready, (2 * l + 2) * NT)
                for c in range(N_OUT):
                    for t in range(NT):
                        eng.wait_ge(sc_done.sem, sc_done.at(l, 2 * c + t + 1))
                        sl = h[:, t, c * 512:c * 512 + 512]
                        eng.scalar_tensor_tensor(sl, sl, ALPHA, ps[:, 2 * c + t, :], ALU.mult, ALU.add)
                eng.drain()
                norm(2 * l + 2, cur_ln[:, 1])
                eng.drain()


_INS = ['x', 'ln0_g', 'ln0_b', 'w_in', 'conv_a_w', 'conv_a_b', 'lru_wa', 'lru_ba', 'lru_wx', 'lru_bx', 'lru_lam',
        'conv_b_w', 'gla_wa2', 'gla_ba2', 'gla_norm_w', 'att_rel_bias', 'w_out', 'ln1_g', 'ln1_b', 'w_rg', 'b_rg',
        'w_re', 'b_re', 'w_gate', 'w_up', 'w_down', 'ln2_g', 'ln2_b']


def kernel(**inputs):
    import numpy as _np
    import concourse.bacc as _bacc
    from concourse import mybir as _mybir
    from concourse.bass_utils import run_bass_kernel_spmd as _run

    nc = _bacc.Bacc("TRN2", target_bir_lowering=False, num_devices=1)
    arrays, args = {}, []
    for name in _INS:
        a = _np.ascontiguousarray(inputs[name])
        arrays[f"in_{name}_dram"] = a
        args.append(nc.dram_tensor(f"in_{name}_dram", a.shape, _mybir.dt.from_np(a.dtype), kind="ExternalInput").ap())
    args.append(nc.dram_tensor("out_0_dram", inputs["x"].shape, _mybir.dt.float32, kind="ExternalOutput").ap())
    trunk(nc, *args)
    r = _run(nc, [arrays], core_ids=[0])
    return r.results[0]["out_0_dram"]
```

```python
from contextlib import ExitStack

import numpy as np
import concourse.bass as bass
from concourse import mybir

F32 = mybir.dt.float32
F32R = mybir.dt.float32r
I32 = mybir.dt.int32
U32 = mybir.dt.uint32
ALU = mybir.AluOpType
ACT = mybir.ActivationFunctionType
AX = mybir.AxisListType

P = 128
BLK = 64
KB = 256
SLOTS = 3
HALVES = 2 * SLOTS
BIG = 3.0e38
NEG = -1.0e30

W_IN = [("dq", 4112), ("dk", 4624), ("dv", 5136), ("cqk", 2560), ("cv", 3072), ("cg", 3584),
        ("ax", 0), ("ag", 512), ("bc", 1536), ("bh", 2048), ("bb", 1024)]
C_A = 4096
RANK = 16

ROWS = {"conv_a_w": (0, 16), "conv_a_b": (16, 4), "lru_ba": (20, 4), "lru_bx": (24, 4), "lru_lam": (28, 4),
        "conv_b_w": (32, 12), "gla_ba2": (44, 2), "gla_norm_w": (46, 4)}
NROWS = 50


class Signal:

    def __init__(self, sem, per_layer):
        self.sem, self.per_layer = sem, per_layer

    def at(self, layer, k):
        return layer * self.per_layer + k


def trunk(nc, x, ln0_g, ln0_b, w_in, conv_a_w, conv_a_b, lru_wa, lru_ba, lru_wx, lru_bx, lru_lam, conv_b_w,
          gla_wa2, gla_ba2, gla_norm_w, att_rel_bias, w_out, ln1_g, ln1_b, w_rg, b_rg, w_re, b_re,
          w_gate, w_up, w_down, ln2_g, ln2_b, out):
    _, T, D = x.shape
    L, E = w_gate.shape[0], w_gate.shape[1]
    F = w_gate.shape[3]
    KD = D // P
    KF = F // P
    NT = T // P
    CH = 64
    NC = T // CH
    HEADS = 4
    G = w_rg.shape[2]
    NR = G + E
    S = 2 * T
    SP_ = S + BLK
    N_IN = len(W_IN)
    N_OUT = D // 512
    FIRST_E = N_IN + N_OUT
    PER_SLOT = (FIRST_E + 3 * E) // SLOTS
    assert (FIRST_E + 3 * E) % SLOTS == 0 and FIRST_E % SLOTS == 0 and T == 256 and D == 2048 and F == 512
    ALPHA = float((2 * L) ** 0.25)
    LN_EPS, RMS_EPS = 1e-5, 1e-6
    LRU_C, TAU = 8.0, 16.0

    ctx = ExitStack()
    with ctx:
        def sb(name, shape, dt=F32):
            return ctx.enter_context(nc.sbuf_tensor(name, shape, dt))

        def semaphore(name):
            return ctx.enter_context(nc.semaphore(name))

        def signal(name, per_layer):
            return Signal(semaphore(name), per_layer)

        def next_address():
            return (nc.sbuf_base + 31) // 32 * 32

        ring_at = next_address()
        ring = sb("ring", [P, SLOTS, KD * 512])
        h = sb("h", [P, NT, D])
        arena_at = next_address()
        arena = sb("arena", [P, 88 * KB])

        def part(name, shape, at):
            return nc.alloc_sbuf_tensor_at(name, shape, F32R, offset=at)

        def area(kib, words):
            return arena[:, kib * KB:kib * KB + words]

        def unit(kib):
            return area(kib, 1024)

        def blocks(ap, n):
            return ap.rearrange("p (b t) -> p b t", b=n)

        hT = area(0, KD * T).rearrange("p (k t) -> p k t", k=KD)
        mixT = area(16, KD * T).rearrange("p (k t) -> p k t", k=KD)
        a_qT, a_kT, a_v, a_H = unit(32), unit(36), unit(40), unit(44)
        a_P = blocks(area(48, HEADS * 384), HEADS)
        a_PT = blocks(area(54, HEADS * 384), HEADS)
        c_qk, c_v, c_g = unit(60), unit(64), unit(68)
        c_bcum, c_t1 = area(72, 512), area(74, 512)
        c_qd, c_ki, c_ke = area(76, 512), area(78, 512), area(80, 512)
        c_aT, c_wa2 = area(82, T), area(83, 256)
        c_wca = area(84, KD * 32).rearrange("p (k r) -> p k r", k=KD)
        c_keT = area(86, 512).rearrange("p (t c) -> p t c", t=NT)
        c_scT = blocks(unit(32), 8)
        c_state = area(36, 3 * 256).rearrange("p (n b v) -> p n b v", n=3, b=2)
        c_sq, c_rs = unit(44), unit(48)
        r_x, r_g, r_u, r_r, r_i = unit(52), unit(56), unit(60), unit(40), unit(76)
        r_w = area(80, 1024).rearrange("p (m h j) -> p m h j", m=2, h=HEADS)
        r_t = unit(32)
        b_c, b_h, b_cv, b_p = unit(64), unit(68), unit(72), unit(36)
        ring_lo = part("ring_lo", [P, SLOTS, KD, 512], ring_at)
        mix_lo = part("mix_lo", [P, KD, T], arena_at + 16 * 1024)
        mix_hi = part("mix_hi", [P, KD, T], arena_at + 36 * 1024)
        w_hi = [part("w_hi_0", [P, 8, 512], arena_at), part("w_hi_1", [P, 8, 512], arena_at + 56 * 1024)]
        xgT = area(0, KD * SP_).rearrange("p (k s) -> p k s", k=KD)
        yT = area(36, KD * SP_).rearrange("p (k s) -> p k s", k=KD)
        ySort = area(0, 4 * D).rearrange("p (b n) -> p b n", b=4)
        hot = area(36, 2 * S).rearrange("p (t s) -> p t s", t=NT)
        hotw = area(40, 2 * S).rearrange("p (t s) -> p t s", t=NT)
        xe = area(72, KD * BLK).rearrange("p (k s) -> p k s", k=KD)
        hmid, sgate = area(76, 256), area(77, 256)
        hmT = area(82, 2 * P).rearrange("p (q n) -> p q n", q=2)
        yraw = area(83, 1024)
        pw = area(78, 4 * T).rearrange("p (b t) -> p b t", b=4)
        gb = area(56, 2 * D).rearrange("p (m n) -> p m n", m=2)
        par_rows = area(32, P)
        ident, ones, before, anti = sb("ident", [P, P]), sb("ones", [P, P]), sb("before", [P, P]), sb("anti", [P, P])
        causal = sb("causal", [P, P])
        lo_row, hi_row = sb("lo_row", [1, P]), sb("hi_row", [1, P])
        par = sb("par", [P, L, NROWS])
        cs, csn = sb("cs", [P, L, 4]), sb("csn", [P, L, 4])
        cur, cur_cs = sb("cur", [P, NROWS]), sb("cur_cs", [P, 2, 4])
        cur_ln = sb("cur_ln", [P, 2, 2, KD])
        sp = sb("sp", [P, 4, L * 4])
        lnc = sb("lnc", [P, 1 + 2 * L, 2, KD])
        wr = area(52, KD * 32).rearrange("p (k n) -> p k n", k=KD)
        lgp = area(44, T)
        fold = sb("fold", [P, 32])
        br = area(54, NR)
        desc = sb("desc", [P, 4])
        slot_iota = sb("slot_iota", [P, S], mybir.dt.int16)
        stats = sb("stats", [P, NT, 4, 6])
        mv = sb("mv", [P, NT, 2])
        rstd = sb("rstd", [P, NT, 2])
        nmax, rsum = sb("nmax", [P, 2, HEADS]), sb("rsum", [P, 2, HEADS])
        blast = sb("blast", [P, 8])
        def small(at, shape):
            n = int(np.prod(shape))
            ap = arena[:, 48 * KB + at:48 * KB + at + n]
            if len(shape) == 2:
                return ap.rearrange("p (a b) -> p a b", b=shape[1])
            return ap.rearrange("p (a b c) -> p a b c", b=shape[1], c=shape[2])

        lg = small(0, (NT, NR))
        gmax, rk, rkm, goh = small(64, (NT, 1)), small(72, (NT, 4)), small(80, (NT, 1)), small(88, (NT, 4))
        t16, eg, oh = small(96, (NT, 16)), small(128, (NT, 4)), small(136, (2, NT, 4))
        emax = small(152, (2, NT, 1))
        ex = small(160, (NT, 5))
        gval, wts = small(176, (NT, 1)), small(184, (2, NT, 1))
        M = small(192, (3, NT, 16))
        pos, pos12 = small(320, (NT, 16)), small(352, (2, NT, 1))
        tab = small(384, (3, 16))
        scn = small(448, (2, 16))
        carry = sb("carry", [P, 1])
        tabi = sb("tabi", [P, 4, 16], I32)

        ps = ctx.enter_context(nc.psum_tensor("ps", [P, 8, 512], F32))

        def banks(b, n):
            return ps[:, b:b + n, :].rearrange("p b n -> p (b n)")

        def slab(slot):
            return ring[:, slot, :].rearrange("p (k n) -> p k n", k=KD)

        def slab_down(slot):
            return ring[:, slot, :].rearrange("p (k n) -> p k n", k=KF)

        slab_loaded = [[semaphore(f"slab_loaded_{s}{i}") for i in range(2)] for s in range(SLOTS)]
        half_used = semaphore("half_used")
        x_loaded = [semaphore(f"x_loaded_{t}") for t in range(NT)]
        par_loaded, lnc_loaded, lnc0_loaded = semaphore("par_loaded"), semaphore("lnc_loaded"), semaphore("lnc0_loaded")
        small_loaded = signal("small_loaded", 16 * 6)
        pads_ready = semaphore("pads_ready")
        router_loaded = signal("router_loaded", 16 * 4)
        lru_loaded = signal("lru_loaded", 16 * 2)
        gb0_loaded = semaphore("gb0_loaded")
        gb1_loaded, gb2_loaded = signal("gb1_loaded", 32), signal("gb2_loaded", 32)
        stored = semaphore("stored")
        consts = semaphore("consts")
        par_T, par_ready = semaphore("par_T"), semaphore("par_ready")
        sp_in, sp_exp, cs_ready = semaphore("sp_in"), semaphore("sp_exp"), semaphore("cs_ready")
        var_ready, std_ready, xn_ready = (semaphore(n) for n in ("var_ready", "std_ready", "xn_ready"))
        xnT_done, hT_act, hT_dve = (semaphore(n) for n in ("xnT_done", "hT_act", "hT_dve"))
        h_ready = semaphore("h_ready")
        acc_full = signal("acc_full", 2 * (N_IN + N_OUT))
        z_evac = signal("z_evac", 2 * (N_IN - 1))
        res_add = signal("res_add", 2 * N_OUT)
        att_scores, att_max, att_exp, att_prob = (signal(n, 1) for n in ("att_scores", "att_max", "att_exp", "att_prob"))
        att_pT, att_pTs, att_o, att_done = (signal(n, 1) for n in ("att_pT", "att_pTs", "att_o", "att_done"))
        ca_done, ca_evac, la_done, la_abs, la_ln, bc_ready = (
            signal(n, 1) for n in ("ca_done", "ca_evac", "la_done", "la_abs", "la_ln", "bc_ready"))
        exps_ready, qk_ready, bl_ready, dec_ready = (signal(n, 1) for n in ("exps_ready", "qk_ready", "bl_ready", "dec_ready"))
        ke_T, ke_evac, gsc_done, gsc_evac = (signal(n, 1) for n in ("ke_T", "ke_evac", "gsc_done", "gsc_evac"))
        kv_done, state_ready, go_done, sq_ready, ms_done, ms_sqrt, gla_done = (
            signal(n, 1) for n in ("kv_done", "state_ready", "go_done", "sq_ready", "ms_done", "ms_sqrt", "gla_done"))
        u_ready, gates_done, sig_ready, at_ready, om_ready, mult_ready, lru_done, gates_free = (
            signal(n, 1) for n in ("u_ready", "gates_done", "sig_ready", "at_ready", "om_ready", "mult_ready",
                                   "lru_done", "gates_free"))
        mixb_ready = signal("mixb_ready", 2)
        mix_rounded, mix_split = signal("mix_rounded", 2), signal("mix_split", 2)
        w_rounded, w_split, w_used = (signal(n, 2 * N_OUT) for n in ("w_rounded", "w_split", "w_used"))
        lgp_done, lgp_ready = signal("lgp_done", 1), signal("lgp_ready", 1)
        fold_ready = semaphore("fold_ready")
        logits_done, ex_in, ex_ready, m_ready, ranks_done, tab_ready, hot_ready = (
            signal(n, 1) for n in ("logits_done", "ex_in", "ex_ready", "m_ready", "ranks_done", "tab_ready", "hot_ready"))
        pwT_done, pw_ready = (signal(n, 1) for n in ("pwT_done", "pw_ready"))
        cur_ready = semaphore("cur_ready")
        gath_done = signal("gath_done", KD)
        gath_act, gath_dve = signal("gath_act", KD // 2), signal("gath_dve", KD // 2)
        xe_ready, gu_done, sg_ready, hm_ready, hmT_done, hmT_ready, y_done, yraw_ready, yt_done, y_evac = (
            semaphore(n) for n in ("xe_ready", "gu_done", "sg_ready", "hm_ready", "hmT_done", "hmT_ready", "y_done",
                                   "yraw_ready", "yt_done", "y_evac"))
        yS_done = signal("yS_done", 16)
        yS_act, yS_dve = signal("yS_act", 8), signal("yS_dve", 8)
        sc_done, ffn_add = signal("sc_done", 2 * N_OUT), signal("ffn_add", 2 * N_OUT)

        block = ctx.enter_context(nc.Block())

        def expert_row(eng, row, e):
            hi = {0: S, 1: T // BLK, 2: 4096}[row]
            return eng.value_load(tabi[0:1, row, bass.ds(e, 1)], min_val=1 if row == 1 else 0, max_val=hi)

        def bank_order(head):
            return (head % 2) * 2 + head // 2

        def block_start(first, j):
            return nc.s_assert_within(first + j * BLK, 0, S, skip_runtime_bounds_check_because=
                                      "a block starts at or before its expert's last slot")

        @block.sync
        def _(sp_eng):
            eng = sp_eng

            def load(l, slab_index, slot, halves):
                eng.wait_ge(half_used, l * (2 * (FIRST_E + 3 * E)) + (2 * slab_index + 2))
                for i, (dst, src) in enumerate(halves):
                    eng.dma_start(dst, src()).then_inc(slab_loaded[slot][i], 16)

            for t in range(NT):
                eng.dma_start(h[:, t, :], x[0, t * P:t * P + P, :]).then_inc(x_loaded[t], 16)
            with eng.Fori(0, L) as l:
                for s, (_, c0) in enumerate(W_IN):
                    src = w_in[bass.ds(l, 1), :, c0:c0 + 512].rearrange("o (p k) n -> p (o k) n", k=KD)
                    eng.wait_ge(half_used, l * (2 * (FIRST_E + 3 * E)) + max(2 * s + 2, 4))
                    for i in (1, 0):
                        eng.dma_start(slab(s % SLOTS)[:, 8 * i:8 * i + 8, :], src[:, 8 * i:8 * i + 8, :]
                                      ).then_inc(slab_loaded[s % SLOTS][i], 16)
                for c in range(N_OUT):
                    s = N_IN + c
                    src = w_out[bass.ds(l, 1), :, c * 512:c * 512 + 512].rearrange("o (k p) n -> p (o k) n", p=P)
                    eng.wait_ge(half_used, l * (2 * (FIRST_E + 3 * E)) + (2 * s + 2))
                    for i in (1, 0):
                        eng.dma_start(slab(s % SLOTS)[:, 8 * i:8 * i + 8, :], src[:, 8 * i:8 * i + 8, :]
                                      ).then_inc(slab_loaded[s % SLOTS][i], 16)

                def load_expert(e, first):
                    before_it = l * (2 * (FIRST_E + 3 * E)) + 2 * (FIRST_E + 3 * e)
                    for i in range(2):
                        eng.wait_ge(half_used, before_it + (4 if first else 2 * i + 2))
                        for m, w in enumerate((w_gate, w_up)):
                            src = w.rearrange("l e d f -> (l e) d f")[bass.ds(l * E + e, 1)].rearrange(
                                "o (p k) n -> p (o k) n", k=KD)
                            eng.dma_start(slab(m)[:, 8 * i:8 * i + 8, :], src[:, 8 * i:8 * i + 8, :]
                                          ).then_inc(slab_loaded[m][i], 16)
                    src = w_down.rearrange("l e f d -> (l e) f d")[bass.ds(l * E + e, 1)].rearrange(
                        "o (k p) n -> p (o k) n", p=P)
                    load(l, FIRST_E + 3 * e + 2, 2, [(slab_down(2)[:, 2 * i:2 * i + 2, :], lambda i=i: src[:, 2 * i:2 * i + 2, :])
                                                     for i in range(2)])

                load_expert(0, True)
                with eng.Fori(1, E) as e:
                    load_expert(e, False)
            for t in range(NT):
                eng.wait_ge(h_ready, NT * 2 * L + t + 1)
                eng.dma_start(out[0, t * P:t * P + P, :], h[:, t, :]).then_inc(stored, 16)
            eng.wait_ge(stored, 16 * NT)

        @block.gpsimd
        def _(eng):
            for t in (ident, before, anti, lo_row, hi_row):
                eng.memset(t[:], 0.0)
            eng.memset(causal[:], 1.0)
            eng.memset(ones[:], 1.0)
            eng.memset(carry[:], 0.0)
            eng.drain()
            eng.memset(lo_row[:, 0:CH], NEG)
            eng.memset(hi_row[:, CH:P], 1.0)
            eng.affine_select(out=ident[:], in_=ident[:], compare_op=ALU.not_equal, fill=1.0, base=0,
                              pattern=[[-1, P]], channel_multiplier=1)
            eng.affine_select(out=anti[:], in_=anti[:], compare_op=ALU.not_equal, fill=1.0, base=-(P - 1),
                              pattern=[[1, P]], channel_multiplier=1)
            eng.affine_select(out=before[:], in_=before[:], compare_op=ALU.is_ge, fill=1.0, base=0,
                              pattern=[[-1, P]], channel_multiplier=1)
            eng.affine_select(out=causal[:], in_=causal[:], compare_op=ALU.is_ge, fill=0.0, base=0,
                              pattern=[[1, P]], channel_multiplier=-1)
            eng.iota(slot_iota[:], pattern=[[1, S]], base=0, channel_multiplier=0,
                     allow_small_or_imprecise_dtypes=True)
            eng.iota(desc[:], pattern=[[-1, 4]], base=4, channel_multiplier=0,
                     allow_small_or_imprecise_dtypes=True)
            eng.drain()
            eng.affine_select(out=causal[:, CH:P], in_=causal[:, CH:P], compare_op=ALU.is_ge, fill=0.0, base=-CH,
                              pattern=[[0, CH]], channel_multiplier=1).then_inc(consts, 1)

            with eng.Fori(0, L) as l:
                eng.wait_ge(gb1_loaded.sem, gb1_loaded.at(l, 32))
                eng.wait_ge(gath_done.sem, gath_done.at(l, KD))
                for t in range(NT):
                    eng.tensor_tensor(h[:, t, :], h[:, t, :], gb[:, 0, :], ALU.mult)
                eng.drain()
                for t in range(NT):
                    eng.tensor_tensor(h[:, t, :], h[:, t, :], gb[:, 1, :], ALU.add).then_inc(h_ready, 1)

        def norm_T_dyn(eng, l, second):
            eng.wait_ge(var_ready, 2 * l + 2 + second)
            eng.activation(rstd[:, :, 0], rstd[:, :, 1], ACT.Sqrt).then_inc(std_ready, 1)
            for c in range(0, 8, 2):
                eng.wait_ge(xnT_done, (2 * l + 1 + second) * 8 + c + 1)
                for k in (2 * c, 2 * c + 1):
                    last = eng.activation(hT[:, k, :], ps[:, c, (k % 2) * T:(k % 2) * T + T], ACT.Identity,
                                          bias=cur_ln[:, second, 1, k:k + 1],
                                          scale=cur_ln[:, second, 0, k:k + 1])
                last.then_inc(hT_act, 1)

        @block.scalar
        def _(eng):
            for m, v in enumerate((ln0_g, ln0_b)):
                eng.dma_start(lnc[:, 0, m, :], v.rearrange("(p k) -> p k", k=KD)).then_inc(lnc0_loaded, 16)
            for l in range(L):
                for name, ap in (("conv_a_w", conv_a_w), ("conv_b_w", conv_b_w)):
                    r0, n = ROWS[name]
                    eng.dma_start(par_rows[l * NROWS + r0:l * NROWS + r0 + n, :],
                                  ap[l].rearrange("k (b c) -> (k b) c", c=P)).then_inc(par_loaded, 16)
                for name, ap in (("conv_a_b", conv_a_b), ("lru_ba", lru_ba), ("lru_bx", lru_bx), ("lru_lam", lru_lam),
                                 ("gla_ba2", gla_ba2), ("gla_norm_w", gla_norm_w)):
                    r0, n = ROWS[name]
                    eng.dma_start(par_rows[l * NROWS + r0:l * NROWS + r0 + n, :],
                                  ap[l].rearrange("(b c) -> b c", c=P)).then_inc(par_loaded, 16)
            for m, v in enumerate((ln0_g, ln0_b)):
                eng.dma_start(gb[:, m, :], v.rearrange("(o n) -> o n", o=1).to_broadcast([P, D])).then_inc(gb0_loaded, 16)
            eng.drain().then_inc(y_evac, 1)
            eng.wait_ge(var_ready, 1)
            eng.activation(rstd[:, :, 0], rstd[:, :, 1], ACT.Sqrt).then_inc(std_ready, 1)
            eng.wait_ge(lnc0_loaded, 32)
            for c in range(0, 8, 2):
                eng.wait_ge(xnT_done, c + 1)
                for k in (2 * c, 2 * c + 1):
                    last = eng.activation(hT[:, k, :], ps[:, c, (k % 2) * T:(k % 2) * T + T], ACT.Identity,
                                          bias=lnc[:, 0, 1, k:k + 1], scale=lnc[:, 0, 0, k:k + 1])
                last.then_inc(hT_act, 1)
            vectors = []
            for l in range(L):
                vectors += [(ln1_g[l], ln1_b[l]), (ln2_g[l], ln2_b[l])]
            for n, pair in enumerate(vectors):
                for m, v in enumerate(pair):
                    eng.dma_start(lnc[:, n + 1, m, :], v.rearrange("(p k) -> p k", k=KD)).then_inc(lnc_loaded, 16)
            eng.wait_ge(sp_in, 1)
            eng.activation(sp[:, 1, :], sp[:, 1, :], ACT.Exp).then_inc(sp_exp, 1)

            with eng.Fori(0, L) as l:
                eng.wait_ge(h_ready, (2 * l + 1) * NT)
                rb = att_rel_bias[bass.ds(l, 1)]
                src = bass.AP(tensor=rb.tensor, offset=rb.offset + P + 1,
                              ap=[[1, P], [att_rel_bias.shape[2], HEADS], [1, T]])
                eng.dma_start(blocks(a_H, HEADS), src).then_inc(small_loaded.sem, 16)
                eng.wait_ge(pads_ready, l + 1)
                for c in range(4):
                    eng.dma_start(c_wa2[32 * c:32 * c + RANK, :], gla_wa2[bass.ds(l, 1)].rearrange("o r c -> (o r) c")
                                  ).then_inc(small_loaded.sem, 16)
                eng.dma_start(c_wca[:, :, 0:RANK], w_in[bass.ds(l, 1), :, C_A:C_A + RANK].rearrange("o (p k) n -> p (o k) n", k=KD)
                              ).then_inc(small_loaded.sem, 16)

                dest = {"dq": a_qT, "dk": a_kT, "dv": a_v, "cqk": c_qk, "cv": c_v, "cg": c_g, "ax": r_x, "ag": r_g,
                        "bc": b_c, "bh": b_h}

                def evacuate(s, func=ACT.Copy, scale=1.0):
                    d = dest[W_IN[s][0]]
                    for i in range(2):
                        eng.wait_ge(acc_full.sem, acc_full.at(l, 2 * s + i + 1))
                        eng.activation(d[:, i * 512:i * 512 + 512], ps[:, i, :], func, scale=scale
                                       ).then_inc(z_evac.sem, 1)

                evacuate(0, scale=float(P) ** -0.5)
                evacuate(1)
                evacuate(2)
                evacuate(3)
                eng.wait_ge(att_max.sem, att_max.at(l, 1))
                for hd in range(HEADS):
                    eng.activation(a_P[:, hd, 0:P], ps[:, 2 + hd, 0:P], ACT.Exp, bias=nmax[:, 0, hd:hd + 1],
                                   accum_out=rsum[:, 0, hd:hd + 1])
                    last = eng.activation(a_P[:, hd, P:384], ps[:, 2 + hd, P:384], ACT.Exp, bias=nmax[:, 1, hd:hd + 1],
                                          accum_out=rsum[:, 1, hd:hd + 1])
                last.then_inc(att_exp.sem, 1)
                evacuate(4)
                eng.wait_ge(att_pT.sem, att_pT.at(l, 1))
                eng.activation(a_PT, ps[:, 2:6, 0:384], ACT.Copy).then_inc(att_pTs.sem, 1)
                eng.wait_ge(ca_done.sem, ca_done.at(l, 1))
                eng.activation(c_aT, ps[:, 6, 0:T], ACT.Copy).then_inc(ca_evac.sem, 1)
                evacuate(5, ACT.Silu)
                eng.wait_ge(att_o.sem, att_o.at(l, 1))
                eng.activation(mixT[:, 12:16, :].rearrange("p k t -> p (k t)"), banks(6, 2), ACT.Copy
                               ).then_inc(att_done.sem, 1)
                eng.wait_ge(la_abs.sem, la_abs.at(l, 1))
                eng.activation(c_t1, c_t1, ACT.Exp)
                eng.drain()
                eng.activation(c_t1, c_t1, ACT.Ln, bias=1.0).then_inc(la_ln.sem, 1)
                eng.wait_ge(bc_ready.sem, bc_ready.at(l, 1))
                eng.activation(c_qd, c_bcum, ACT.Exp, scale=1.0 / TAU)
                eng.activation(c_ki, c_bcum, ACT.Exp, scale=-1.0 / TAU)
                eng.activation(c_ke, c_t1, ACT.Exp, scale=1.0 / TAU)
                eng.activation(blast[:], c_bcum.rearrange("p (n c) -> p n c", c=CH)[:, :, CH - 1], ACT.Exp,
                               scale=1.0 / TAU).then_inc(exps_ready.sem, 1)
                evacuate(6)
                eng.wait_ge(ke_T.sem, ke_T.at(l, 1))
                eng.activation(c_keT.rearrange("p t c -> p (t c)"), ps[:, 3, :], ACT.Copy).then_inc(ke_evac.sem, 1)
                evacuate(7, ACT.Gelu_apprx_tanh)
                eng.wait_ge(go_done.sem, go_done.at(l, 1))
                eng.activation(c_sq, banks(4, 2), ACT.Square).then_inc(sq_ready.sem, 1)
                for m, w in enumerate((lru_wa, lru_wx)):
                    eng.dma_start(r_w[:, m, :, :], w[bass.ds(l, 1)].rearrange("o h i j -> i (o h) j")
                                  ).then_inc(lru_loaded.sem, 16)
                eng.wait_ge(ms_done.sem, ms_done.at(l, 1))
                eng.activation(c_rs, banks(2, 2), ACT.Identity, bias=RMS_EPS, scale=1.0 / P)
                eng.drain()
                eng.activation(c_rs, c_rs, ACT.Sqrt).then_inc(ms_sqrt.sem, 1)
                evacuate(8)
                eng.wait_ge(gla_done.sem, gla_done.at(l, 1))
                eng.wait_ge(cur_ready, l + 1)
                eng.wait_ge(gates_done.sem, gates_done.at(l, 1))
                for m, (dst, name) in enumerate(((r_r, "lru_ba"), (r_i, "lru_bx"))):
                    for b in range(4):
                        col = ROWS[name][0] + b
                        last = eng.activation(dst[:, b * T:b * T + T], banks(2 + 4 * m, 2)[:, b * T:b * T + T],
                                              ACT.Sigmoid, bias=cur[:, col:col + 1])
                last.then_inc(gates_free.sem, 1)
                eng.drain()
                for b in range(4):
                    eng.activation(r_t[:, b * T:b * T + T], r_r[:, b * T:b * T + T], ACT.Tanh,
                                   scale=cur_cs[:, 0, b:b + 1])
                eng.drain()
                for b in range(4):
                    last = eng.activation(r_r[:, b * T:b * T + T], r_r[:, b * T:b * T + T], ACT.Exp,
                                          scale=cur_cs[:, 1, b:b + 1])
                last.then_inc(at_ready.sem, 1)
                evacuate(9)
                eng.wait_ge(om_ready.sem, om_ready.at(l, 1))
                eng.activation(r_t, r_t, ACT.Sqrt).then_inc(mult_ready.sem, 1)
                def round_w(c, i):
                    s = N_IN + c
                    eng.wait_ge(slab_loaded[s % SLOTS][i], 16 * (l * PER_SLOT + s // SLOTS + 1))
                    eng.activation(w_hi[i][:], slab(s % SLOTS)[:, 8 * i:8 * i + 8, :], ACT.Copy).then_inc(w_rounded.sem, 1)

                eng.wait_ge(lru_done.sem, lru_done.at(l, 1))
                eng.activation(mix_hi[:, 0:4, :], mixT[:, 0:4, :], ACT.Copy)
                eng.activation(mix_hi[:, 8:16, :], mixT[:, 8:16, :], ACT.Copy).then_inc(mix_rounded.sem, 1)
                round_w(0, 1)
                eng.wait_ge(mixb_ready.sem, mixb_ready.at(l, 2))
                eng.activation(mix_hi[:, 4:8, :], mixT[:, 4:8, :], ACT.Copy).then_inc(mix_rounded.sem, 1)
                round_w(0, 0)
                eng.dma_start(wr[:, :, 0:G], w_rg[bass.ds(l, 1)].rearrange("o (p k) g -> p (o k) g", k=KD)
                              ).then_inc(router_loaded.sem, 16)
                eng.dma_start(wr[:, :, G:NR], w_re[bass.ds(l, 1)].rearrange("o (p k) g -> p (o k) g", k=KD)
                              ).then_inc(router_loaded.sem, 16)
                eng.dma_start(br[:, 0:G], b_rg[bass.ds(l, 1)].to_broadcast([P, G])).then_inc(router_loaded.sem, 16)
                eng.dma_start(br[:, G:NR], b_re[bass.ds(l, 1)].to_broadcast([P, E])).then_inc(router_loaded.sem, 16)

                for c in range(1, N_OUT):
                    for n, i in enumerate((1, 0)):
                        eng.wait_ge(w_used.sem, w_used.at(l, 2 * (c - 1) + n + 1))
                        round_w(c, i)
                eng.wait_ge(w_used.sem, w_used.at(l, 2 * N_OUT))
                for m, v in enumerate((ln1_g, ln1_b)):
                    eng.dma_start(gb[:, m, :], v[bass.ds(l, 1)].to_broadcast([P, D])).then_inc(gb1_loaded.sem, 16)

                norm_T_dyn(eng, l, 0)
                eng.wait_ge(lgp_done.sem, lgp_done.at(l, 1))
                eng.activation(lgp, ps[:, 0, 0:T], ACT.Copy).then_inc(lgp_ready.sem, 1)
                eng.wait_ge(ex_in.sem, ex_in.at(l, 1))
                eng.activation(ex, ex, ACT.Exp).then_inc(ex_ready.sem, 1)
                for k in range(0, KD, 2):
                    eng.wait_ge(gath_done.sem, gath_done.at(l, k + 1))
                    eng.activation(xgT[:, k, 0:S], ps[:, k % 8, :], ACT.Identity,
                                   bias=cur_ln[:, 0, 1, k:k + 1], scale=cur_ln[:, 0, 0, k:k + 1]
                                   ).then_inc(gath_act.sem, 1)
                eng.wait_ge(pwT_done.sem, pwT_done.at(l, 1))
                eng.activation(pw.rearrange("p b t -> p (b t)"), banks(6, 2), ACT.Copy).then_inc(pw_ready.sem, 1)
                with eng.Fori(0, E) as e:
                    first, n, g0 = expert_row(eng, 0, e), expert_row(eng, 1, e), expert_row(eng, 2, e)
                    with eng.Fori(0, n) as j:
                        eng.wait_ge(gu_done, g0 + j + 2)
                        eng.activation(sgate, ps[:, 0, 0:256], ACT.Silu).then_inc(sg_ready, 1)
                        eng.wait_ge(hmT_done, g0 + j + 1)
                        eng.activation(hmT.rearrange("p q n -> p (q n)"), ps[:, 1, 0:256], ACT.Copy
                                       ).then_inc(hmT_ready, 1)
                        eng.wait_ge(y_done, g0 + j + 1)
                        eng.activation(yraw, banks(2, 2), ACT.Copy).then_inc(yraw_ready, 1)
                        eng.wait_ge(yt_done, g0 + j + 1)
                        eng.wait_ge(h_ready, (2 * l + 2) * NT)
                        dst = yT.rearrange("p (i c q) s -> p c i q s", i=2, c=2)
                        src = banks(4, 2).rearrange("p (i q c s) -> p c i q s", i=2, q=4, c=2)
                        for c in range(2):
                            last = eng.activation(dst[:, c, :, :, bass.ds(block_start(first, j), BLK)], src[:, c], ACT.Copy)
                        last.then_inc(y_evac, 1)
                for c in range(0, 16, 2):
                    eng.wait_ge(yS_done.sem, yS_done.at(l, c + 1))
                    eng.activation(ySort[:, c // 4, (c % 4) * 512:(c % 4) * 512 + 512], ps[:, c % 8, :], ACT.Copy
                                   ).then_inc(yS_act.sem, 1)
                eng.wait_ge(yS_done.sem, yS_done.at(l, 16))
                for m, v in enumerate((ln2_g, ln2_b)):
                    eng.dma_start(gb[:, m, :], v[bass.ds(l, 1)].to_broadcast([P, D])).then_inc(gb2_loaded.sem, 16)
                norm_T_dyn(eng, l, 1)

        @block.tensor
        def _(eng):
            def turn(n):
                eng.wait_ge(xn_ready, (n + 1) * NT)
                for c in range(8):
                    for k in (2 * c, 2 * c + 1):
                        for t in range(NT):
                            o = (k % 2) * T + t * P
                            last = eng.transpose(ps[:, c, o:o + P], h[:, t, k:D:KD], ident[:])
                    last.then_inc(xnT_done, 1)

            eng.drain().then_inc(gu_done, 1)
            eng.wait_ge(consts, 1)
            eng.wait_ge(par_loaded, 16 * 8 * L)
            eng.transpose(ps[:, 0, 0:L * NROWS], par_rows[0:L * NROWS, :], ident[0:L * NROWS, 0:L * NROWS]
                          ).then_inc(par_T, 1)
            eng.drain().then_inc(half_used, HALVES)
            eng.wait_ge(par_ready, 1)
            turn(0)

            def project(l, s, token_major):
                slot = s % SLOTS
                w = slab(slot)
                n_load = l * PER_SLOT + s // SLOTS + 1
                eng.wait_ge(slab_loaded[slot][0], 16 * n_load)
                eng.wait_ge(slab_loaded[slot][1], 16 * n_load)
                for i in range(2):
                    if s >= 1:
                        eng.wait_ge(z_evac.sem, z_evac.at(l, 2 * (s - 1) + i + 1))
                    if token_major:
                        for k in range(KD):
                            last = eng.matmul(ps[:, i, :], hT[:, k, i * P:i * P + P], w[:, k, :],
                                              start=(k == 0), stop=(k == KD - 1))
                    else:
                        for b in (2 * i, 2 * i + 1):
                            for k in range(KD):
                                last = eng.matmul(ps[:, i, (b % 2) * T:(b % 2) * T + T], w[:, k, b * P:b * P + P],
                                                  hT[:, k, :], start=(k == 0), stop=(k == KD - 1))
                    last.then_inc(acc_full.sem, 1)
                return last

            def release():
                eng.drain().then_inc(half_used, 2)

            with eng.Fori(0, L) as l:
                eng.wait_ge(hT_act, (2 * l + 1) * 4)
                eng.wait_ge(hT_dve, (2 * l + 1) * 4)
                for s in range(4):
                    project(l, s, W_IN[s][0] == "dv")
                    release()
                eng.wait_ge(small_loaded.sem, small_loaded.at(l, 96))
                eng.wait_ge(z_evac.sem, z_evac.at(l, 4))
                qT, kT, band = blocks(a_qT, 4), blocks(a_kT, 4), blocks(a_H, 4)
                for hd in range(HEADS):
                    for t in range(NT):
                        for sbk in range(t + 1):
                            o = ps[:, 2 + hd, (t + sbk) * P:(t + sbk) * P + P]
                            eng.matmul(o, qT[:, hd, t * P:t * P + P], kT[:, hd, sbk * P:sbk * P + P], start=True, stop=False)
                            last = eng.matmul(o, band[:, hd, (t - sbk) * P:(t - sbk) * P + P], anti[:],
                                              start=False, stop=(sbk < t))
                            if sbk == t:
                                last = eng.matmul(o, lo_row[:], hi_row[:], start=False, stop=True)
                last.then_inc(att_scores.sem, 1)
                project(l, 4, True)
                release()
                eng.wait_ge(att_prob.sem, att_prob.at(l, 1))
                for hd in range(HEADS):
                    for c in range(3):
                        last = eng.transpose(ps[:, 2 + hd, c * P:c * P + P], a_P[:, hd, c * P:c * P + P], ident[:])
                last.then_inc(att_pT.sem, 1)
                for k in range(KD):
                    c = 32 * (k % 4)
                    last = eng.matmul(ps[c:c + 32, 6, 0:T], c_wca[:, k, :], hT[:, k, :], start=(k < 4), stop=(k >= KD - 4),
                                      tile_position=(0, c))
                last.then_inc(ca_done.sem, 1)
                project(l, 5, False)
                release()
                eng.wait_ge(att_pTs.sem, att_pTs.at(l, 1))
                eng.wait_ge(ca_evac.sem, ca_evac.at(l, 1))
                eng.wait_ge(z_evac.sem, z_evac.at(l, 6))
                v = blocks(a_v, NT)
                for hd in range(HEADS):
                    o = ps[:, 6 + hd // 2, (hd % 2) * T:(hd % 2) * T + T]
                    eng.matmul(o, v[:, 0, hd * P:hd * P + P], a_PT[:, hd, 0:T], start=True, stop=False)
                    last = eng.matmul(o[:, P:T], v[:, 1, hd * P:hd * P + P], a_PT[:, hd, T:384], start=False, stop=True)
                last.then_inc(att_o.sem, 1)
                for b in range(2):
                    last = eng.matmul(ps[:, 2, b * T:b * T + T], c_wa2[:, b * P:b * P + P], c_aT, start=True, stop=True)
                last.then_inc(la_done.sem, 1)
                project(l, 6, False)
                release()
                eng.wait_ge(qk_ready.sem, qk_ready.at(l, 1))
                for b in range(2):
                    for t in range(NT):
                        last = eng.transpose(ps[:, 3, t * 256 + b * P:t * 256 + b * P + P],
                                             c_ke[:, b * T + t * P:b * T + t * P + P], ident[:])
                last.then_inc(ke_T.sem, 1)
                for par_ in range(2):
                    for b in range(2):
                        r0 = par_ * 64
                        for t in range(NT):
                            c0 = b * T + t * P
                            last = eng.matmul(ps[:, 4 + par_, (b * NT + t) * P:(b * NT + t) * P + P],
                                              c_ki[r0:r0 + 64, c0:c0 + P], c_qd[r0:r0 + 64, c0:c0 + P],
                                              start=True, stop=True)
                last.then_inc(gsc_done.sem, 1)
                project(l, 7, False)
                release()
                eng.wait_ge(ke_evac.sem, ke_evac.at(l, 1))
                eng.wait_ge(att_done.sem, att_done.at(l, 1))
                vv = blocks(c_v, NT)
                for n in range(3):
                    r0 = (n % 2) * CH
                    for b in range(2):
                        last = eng.matmul(ps[:, (6, 7, 2)[n], b * 256:b * 256 + 256],
                                          c_keT[r0:r0 + CH, n // 2, b * P:b * P + P],
                                          vv[r0:r0 + CH, n // 2, b * 256:b * 256 + 256], start=True, stop=True)
                last.then_inc(kv_done.sem, 1)
                eng.wait_ge(gsc_evac.sem, gsc_evac.at(l, 1))
                eng.wait_ge(state_ready.sem, state_ready.at(l, 1))
                for hd in range(HEADS):
                    b, r0 = hd // 2, (hd % 2) * 64
                    for t in range(NT):
                        c0 = b * T + t * P
                        eng.matmul(ps[:, 4 + hd % 2, c0:c0 + P], vv[:, t, hd * P:hd * P + P],
                                   c_scT[:, (hd % 2) * 4 + b * NT + t, :], start=True, stop=False)
                        for n in (2 * t, 2 * t + 1):
                            if n:
                                o0 = b * T + n * CH
                                last = eng.matmul(ps[:, 4 + hd % 2, o0:o0 + CH], c_state[r0:r0 + 64, n - 1, b, :],
                                                  c_qd[r0:r0 + 64, b * T + n * CH:b * T + n * CH + CH],
                                                  start=False, stop=(n % 2 == 1))
                last.then_inc(go_done.sem, 1)
                eng.wait_ge(sq_ready.sem, sq_ready.at(l, 1))
                for b in range(2):
                    last = eng.matmul(ps[:, 2 + b, :], ones[:], c_sq[:, b * 512:b * 512 + 512], start=True, stop=True)
                last.then_inc(ms_done.sem, 1)
                project(l, 8, False)
                release()
                eng.wait_ge(u_ready.sem, u_ready.at(l, 1))
                eng.wait_ge(lru_loaded.sem, lru_loaded.at(l, 32))
                eng.wait_ge(ms_sqrt.sem, ms_sqrt.at(l, 1))
                for m in range(2):
                    for b in range(4):
                        last = eng.matmul(banks(2 + 4 * m, 2)[:, b * T:b * T + T], r_w[:, m, b, :],
                                          r_u[:, b * T:b * T + T], start=True, stop=True)
                last.then_inc(gates_done.sem, 1)
                project(l, 9, False)
                release()
                project(l, 10, False)
                release()

                eng.wait_ge(att_done.sem, att_done.at(l, 1))
                eng.wait_ge(gla_done.sem, gla_done.at(l, 1))
                eng.wait_ge(lru_done.sem, lru_done.at(l, 1))
                eng.wait_ge(gates_free.sem, gates_free.at(l, 1))
                for c in range(N_OUT):
                    s = N_IN + c
                    for n, i in enumerate((1, 0)):
                        eng.wait_ge(w_split.sem, w_split.at(l, 2 * c + n + 1))
                        if c == 0:
                            eng.wait_ge(mix_split.sem, mix_split.at(l, n + 1))
                        for t in range(NT):
                            if n == 0 and c >= 2:
                                eng.wait_ge(res_add.sem, res_add.at(l, 2 * (c - 2) + t + 1))
                            for k in range(8 * i, 8 * i + 8):
                                hi, lo = w_hi[i][:, k % 8, :], ring_lo[:, s % SLOTS, k, :]
                                for j, (m, w) in enumerate(((mix_hi, hi), (mix_hi, lo), (mix_lo, hi))):
                                    last = eng.matmul(ps[:, 2 + 2 * (c % 2) + t, :], m[:, k, t * P:t * P + P], w,
                                                      start=(k == 8 and j == 0), stop=(k == 7 and j == 2))
                            if n == 1:
                                last.then_inc(acc_full.sem, 1)
                        eng.drain().then_inc(w_used.sem, 1)
                        eng.drain().then_inc(half_used, 1)

                turn(2 * l + 1)
                eng.wait_ge(router_loaded.sem, router_loaded.at(l, 64))
                eng.wait_ge(hT_act, (2 * l + 2) * 4)
                eng.wait_ge(hT_dve, (2 * l + 2) * 4)
                for k in range(KD):
                    c = 32 * (k % 4)
                    last = eng.matmul(ps[c:c + 32, 0, 0:T], wr[:, k, :], hT[:, k, :], start=(k < 4), stop=(k >= KD - 4),
                                      tile_position=(0, c))
                last.then_inc(lgp_done.sem, 1)
                eng.wait_ge(lgp_ready.sem, lgp_ready.at(l, 1))
                eng.wait_ge(fold_ready, 1)
                for t in range(NT):
                    last = eng.matmul(ps[:, 2, t * NR:t * NR + NR], lgp[:, t * P:t * P + P], fold[:, 0:NR],
                                      start=True, stop=True)
                last.then_inc(logits_done.sem, 1)
                eng.wait_ge(m_ready.sem, m_ready.at(l, 1))
                eng.matmul(ps[:, 1, 0:16], before[:], M[:, 2, 0, :], start=True, stop=True)
                eng.matmul(ps[:, 1, 16:32], ones[:], M[:, 2, 0, :], start=True, stop=False)
                eng.matmul(ps[:, 1, 16:32], before[:], M[:, 2, 1, :], start=False, stop=True)
                eng.matmul(ps[:, 1, 32:48], ones[:], M[:, 2, 0, :], start=True, stop=False)
                eng.matmul(ps[:, 1, 32:48], ones[:], M[:, 2, 1, :], start=False, stop=True).then_inc(ranks_done.sem, 1)
                eng.wait_ge(hot_ready.sem, hot_ready.at(l, 1))
                for k in range(KD):
                    if k >= 8:
                        if k % 2 == 0:
                            eng.wait_ge(gath_act.sem, gath_act.at(l, (k - 8) // 2 + 1))
                        else:
                            eng.wait_ge(gath_dve.sem, gath_dve.at(l, (k - 8) // 2 + 1))
                    for t in range(NT):
                        last = eng.matmul(ps[:, k % 8, :], h[:, t, k:D:KD], hot[:, t, :], start=(t == 0), stop=(t == NT - 1))
                    last.then_inc(gath_done.sem, 1)
                eng.wait_ge(gath_act.sem, gath_act.at(l, 8))
                eng.wait_ge(gath_dve.sem, gath_dve.at(l, 8))
                for sbk in range(4):
                    for t in range(NT):
                        last = eng.transpose(banks(6, 2)[:, sbk * T + t * P:sbk * T + t * P + P],
                                             hotw[:, t, sbk * P:sbk * P + P], ident[:])
                last.then_inc(pwT_done.sem, 1)

                def expert_block(g, e, last_block):
                    n_load = l * PER_SLOT + FIRST_E // SLOTS + e + 1
                    eng.wait_ge(xe_ready, g + 1)
                    for i in range(2):
                        eng.wait_ge(slab_loaded[0][i], 16 * n_load)
                        eng.wait_ge(slab_loaded[1][i], 16 * n_load)
                        for k in range(8 * i, 8 * i + 8):
                            for c in range(2):
                                last = eng.matmul(ps[64 * c:64 * c + BLK, 0, :], xe[:, k, :],
                                                  ring[:, 0:2, k * 512 + c * 256:k * 512 + c * 256 + 256],
                                                  start=(k == 0), stop=(k == KD - 1))
                        if i == 1:
                            last.then_inc(gu_done, 1)
                        if last_block:
                            release()
                    eng.wait_ge(hm_ready, g + 1)
                    for q in range(2):
                        last = eng.transpose(ps[:, 1, q * P:q * P + P], hmid[:, q * P:q * P + P], ident[:])
                    last.then_inc(hmT_done, 1)
                    eng.wait_ge(hmT_ready, g + 1)
                    for f in range(KF):
                        if f % 2 == 0:
                            eng.wait_ge(slab_loaded[2][f // 2], 16 * n_load)
                        for ch in range(4):
                            r0 = 64 * (ch % 2)
                            last = eng.matmul(ps[r0:r0 + BLK, 2 + ch // 2, :], hmT[:, f % 2, 64 * (f // 2):64 * (f // 2) + BLK],
                                              slab_down(2)[:, f, ch * 512:ch * 512 + 512],
                                              start=(f == 0), stop=(f == KF - 1))
                    last.then_inc(y_done, 1)
                    if last_block:
                        release()
                    eng.wait_ge(yraw_ready, g + 1)
                    eng.wait_ge(y_evac, g + 1)
                    for q in range(8):
                        last = eng.transpose(banks(4, 2)[:, q * P:q * P + P], yraw[:, q * P:q * P + P], ident[:])
                    last.then_inc(yt_done, 1)

                with eng.Fori(0, E) as e:
                    n, g0 = expert_row(eng, 1, e), expert_row(eng, 2, e)
                    with eng.If(n > 1):
                        with eng.Fori(0, n - 1) as j:
                            expert_block(g0 + j, e, False)
                    expert_block(g0 + n - 1, e, True)

                n, g0 = expert_row(eng, 1, E - 1), expert_row(eng, 2, E - 1)
                eng.wait_ge(y_evac, g0 + n + 1)
                for c in range(16):
                    if c >= 8:
                        if c % 2 == 0:
                            eng.wait_ge(yS_act.sem, yS_act.at(l, (c - 8) // 2 + 1))
                        else:
                            eng.wait_ge(yS_dve.sem, yS_dve.at(l, (c - 8) // 2 + 1))
                    for q in range(4):
                        last = eng.transpose(ps[:, c % 8, q * P:q * P + P],
                                             yT[:, (c % 4) * 4 + q, (c // 4) * P:(c // 4) * P + P], ident[:])
                    last.then_inc(yS_done.sem, 1)
                eng.wait_ge(yS_act.sem, yS_act.at(l, 8))
                eng.wait_ge(yS_dve.sem, yS_dve.at(l, 8))
                eng.wait_ge(pw_ready.sem, pw_ready.at(l, 1))
                for c in range(N_OUT):
                    for t in range(NT):
                        for sbk in range(4):
                            last = eng.matmul(ps[:, 2 * c + t, :], pw[:, sbk, t * P:t * P + P],
                                              ySort[:, sbk, c * 512:c * 512 + 512], start=(sbk == 0), stop=(sbk == 3))
                        last.then_inc(sc_done.sem, 1)
                turn(2 * l + 2)

        @block.vector
        def _(eng):
            def tt(o, a, b, op):
                return eng.tensor_tensor(o, a, b, op)

            def ts(o, a, s1, s2, op0, op1=None):
                return eng.tensor_scalar(o, a, s1, s2, op0, op1) if op1 is not None else eng.tensor_scalar(o, a, s1, None, op0)

            def norm(n, gb, vectors_there=None):
                eng.drain()
                for t in range(NT):
                    eng.bn_aggr(mv[:, t, :], stats[:, t, :, :].rearrange("p c s -> p (c s)"))
                eng.drain()
                ts(rstd[:, :, 1], mv[:, :, 1], LN_EPS, None, ALU.add).then_inc(var_ready, 1)
                eng.wait_ge(std_ready, n + 1)
                eng.reciprocal(rstd[:, :, 1], rstd[:, :, 0])
                eng.drain()
                for t in range(NT):
                    ts(h[:, t, :], h[:, t, :], mv[:, t, 0:1], rstd[:, t, 1:2], ALU.subtract, ALU.mult).then_inc(xn_ready, 1)
                if vectors_there:
                    eng.wait_ge(*vectors_there)
                for c in range(1, 8, 2):
                    eng.wait_ge(xnT_done, n * 8 + c + 1)
                    for k in (2 * c, 2 * c + 1):
                        g_, b_ = gb[:, 0, k:k + 1], gb[:, 1, k:k + 1]
                        last = ts(hT[:, k, :], ps[:, c, (k % 2) * T:(k % 2) * T + T], g_, b_, ALU.mult, ALU.add)
                    last.then_inc(hT_dve, 1)

            def affine_h(gb_loaded, value):
                eng.wait_ge(gb_loaded, value)
                for t in range(NT):
                    tt(h[:, t, :], h[:, t, :], gb[:, 0, :], ALU.mult)
                    eng.drain()
                    tt(h[:, t, :], h[:, t, :], gb[:, 1, :], ALU.add).then_inc(h_ready, 1)

            def column(l, name, i):
                return cur[:, ROWS[name][0] + i:ROWS[name][0] + i + 1]

            for t in range(NT):
                eng.wait_ge(x_loaded[t], 16)
                for c in range(4):
                    eng.bn_stats(stats[:, t, c, :], h[:, t, c * 512:c * 512 + 512])
            eng.wait_ge(par_T, 1)
            eng.tensor_copy(par[:].rearrange("p l r -> p (l r)"), ps[:, 0, 0:L * NROWS]).then_inc(par_ready, 1)
            norm(0, lnc[:, 0], (lnc0_loaded, 32))
            affine_h(gb0_loaded, 32)
            eng.drain()
            lam = par[:, :, ROWS["lru_lam"][0]:ROWS["lru_lam"][0] + 4]
            s0, s1, s2, s3 = (sp[:, i, :].rearrange("p (l b) -> p l b", l=L) for i in range(4))
            ts(s0, lam, -1.0, 0.0, ALU.mult, ALU.max)
            eng.scalar_tensor_tensor(s1, lam, -1.0, lam, ALU.mult, ALU.min).then_inc(sp_in, 1)
            eng.wait_ge(sp_exp, 1)
            ts(s2, s1, 2.0, None, ALU.add)
            eng.drain()
            eng.reciprocal(s2, s2)
            eng.drain()
            tt(s1, s1, s2, ALU.mult)
            eng.drain()
            tt(s2, s1, s1, ALU.mult)
            eng.drain()
            ts(s3, s2, 1.0 / 17.0, 1.0 / 15.0, ALU.mult, ALU.add)
            for d in (13.0, 11.0, 9.0, 7.0, 5.0, 3.0, 1.0):
                eng.drain()
                tt(s3, s3, s2, ALU.mult)
                eng.drain()
                ts(s3, s3, 1.0 / d, None, ALU.add)
            eng.drain()
            tt(s3, s3, s1, ALU.mult)
            eng.drain()
            eng.scalar_tensor_tensor(s3, s3, 2.0, s0, ALU.mult, ALU.add)
            eng.drain()
            ts(cs[:], s3, LRU_C, None, ALU.mult)
            ts(csn[:], s3, -LRU_C, None, ALU.mult).then_inc(cs_ready, 1)

            eng.wait_ge(consts, 1)
            eng.tensor_reduce(fold[:], ident[:].rearrange("p (c n) -> p n c", c=4), AX.X, ALU.add).then_inc(fold_ready, 1)
            eng.wait_ge(lnc_loaded, 16 * 4 * L)
            eng.drain()

            with eng.Fori(0, L) as l:
                eng.memset(c_wa2, 0.0)
                eng.memset(c_wca[:, :, RANK:32], 0.0).then_inc(pads_ready, 1)
                eng.wait_ge(hT_act, (2 * l + 1) * 4)
                eng.tensor_copy(cur[:], par[:, bass.ds(l, 1), :].rearrange("p o r -> p (o r)"))
                eng.tensor_copy(cur_cs[:, 0, :], cs[:, bass.ds(l, 1), :].rearrange("p o r -> p (o r)"))
                eng.tensor_copy(cur_cs[:, 1, :], csn[:, bass.ds(l, 1), :].rearrange("p o r -> p (o r)"))
                eng.tensor_copy(cur_ln[:], lnc[:, bass.ds(2 * l + 1, 2), :, :]).then_inc(cur_ready, 1)
                eng.wait_ge(att_scores.sem, att_scores.at(l, 1))
                eng.tensor_reduce(nmax[:, 0, :], ps[:, 2:6, 0:P], AX.X, ALU.max, negate=True)
                eng.tensor_reduce(nmax[:, 1, :], ps[:, 2:6, P:384], AX.X, ALU.max, negate=True).then_inc(att_max.sem, 1)
                eng.wait_ge(att_exp.sem, att_exp.at(l, 1))
                eng.reciprocal(rsum[:], rsum[:])
                eng.drain()
                for hd in range(HEADS):
                    ts(a_P[:, hd, 0:P], a_P[:, hd, 0:P], rsum[:, 0, hd:hd + 1], None, ALU.mult)
                    last = ts(a_P[:, hd, P:384], a_P[:, hd, P:384], rsum[:, 1, hd:hd + 1], None, ALU.mult)
                last.then_inc(att_prob.sem, 1)

                eng.wait_ge(la_done.sem, la_done.at(l, 1))
                for b in range(2):
                    ts(c_bcum[:, b * T:b * T + T], ps[:, 2, b * T:b * T + T], column(l, "gla_ba2", b), None, ALU.add)
                eng.drain()
                eng.scalar_tensor_tensor(c_t1, c_bcum, -1.0, c_bcum, ALU.mult, ALU.min).then_inc(la_abs.sem, 1)
                eng.wait_ge(la_ln.sem, la_ln.at(l, 1))
                eng.scalar_tensor_tensor(c_t1, c_bcum, 0.0, c_t1, ALU.min, ALU.subtract)
                eng.drain()
                for i in range(8):
                    sl = slice(i * CH, i * CH + CH)
                    eng.tensor_tensor_scan(c_bcum[:, sl], c_t1[:, sl], c_t1[:, sl], 0.0, ALU.add, ALU.bypass)
                eng.drain()
                bc3 = c_bcum.rearrange("p (n c) -> p n c", c=CH)
                tt(c_t1.rearrange("p (n c) -> p n c", c=CH), bc3[:, :, CH - 1:CH].to_broadcast([P, 8, CH]), bc3,
                   ALU.subtract).then_inc(bc_ready.sem, 1)
                eng.wait_ge(exps_ready.sem, exps_ready.at(l, 1))
                eng.scalar_tensor_tensor(c_qd, c_qk[:, 0:512], 0.125, c_qd, ALU.mult, ALU.mult)
                tt(c_ki, c_ki, c_qk[:, 512:1024], ALU.mult)
                tt(c_ke, c_ke, c_qk[:, 512:1024], ALU.mult).then_inc(qk_ready.sem, 1)
                eng.drain()
                eng.wait_ge(z_evac.sem, z_evac.at(l, 14))
                u, xin = blocks(r_u, 4), blocks(r_x, 4)
                for b in range(4):
                    ts(u[:, b, :], xin[:, b, :], column(l, "conv_a_w", 12 + b), column(l, "conv_a_b", b), ALU.mult, ALU.add)
                for d in range(1, 4):
                    eng.drain()
                    for b in range(4):
                        last = eng.scalar_tensor_tensor(u[:, b, d:T], xin[:, b, 0:T - d],
                                                        column(l, "conv_a_w", (3 - d) * 4 + b), u[:, b, d:T],
                                                        ALU.mult, ALU.add)
                last.then_inc(u_ready.sem, 1)
                eng.wait_ge(gsc_done.sem, gsc_done.at(l, 1))
                eng.memset(c_scT, 0.0)
                eng.drain()
                mask = causal[:].bitcast(U32).rearrange("p (o t) -> p o t", o=1).to_broadcast([P, 4, P])
                for i in range(2):
                    last = eng.copy_predicated(c_scT[:, 4 * i:4 * i + 4, :], mask,
                                               ps[:, 4 + i, :].rearrange("p (j t) -> p j t", j=4))
                last.then_inc(gsc_evac.sem, 1)
                eng.wait_ge(kv_done.sem, kv_done.at(l, 1))
                for n in range(3):
                    bank = (6, 7, 2)[n]
                    for b in range(2):
                        for i in range(2):
                            r = slice(64 * i, 64 * i + 64)
                            src = ps[r, bank, b * 256 + i * P:b * 256 + i * P + P]
                            if n == 0:
                                last = eng.tensor_copy(c_state[r, 0, b, :], src)
                            else:
                                last = eng.scalar_tensor_tensor(c_state[r, n, b, :], c_state[r, n - 1, b, :],
                                                                blast[r, b * 4 + n:b * 4 + n + 1], src, ALU.mult, ALU.add)
                    if n < 2:
                        eng.drain()
                last.then_inc(state_ready.sem, 1)
                eng.wait_ge(ms_sqrt.sem, ms_sqrt.at(l, 1))
                eng.reciprocal(c_rs, c_rs)
                eng.drain()
                tt(c_rs, c_rs, banks(4, 2), ALU.mult)
                eng.drain()
                for b in range(4):
                    last = eng.scalar_tensor_tensor(mixT[:, 8 + b, :], c_rs[:, bank_order(b) * T:bank_order(b) * T + T],
                                                    column(l, "gla_norm_w", b),
                                                    c_g[:, b * T:b * T + T], ALU.mult, ALU.mult)
                last.then_inc(gla_done.sem, 1)

                eng.wait_ge(at_ready.sem, at_ready.at(l, 1))
                tt(r_i, r_i, r_u, ALU.mult)
                ts(r_x, r_t, 1.0, None, ALU.add)
                eng.drain()
                eng.reciprocal(r_x, r_x)
                eng.drain()
                eng.scalar_tensor_tensor(r_t, r_t, 2.0, r_x, ALU.mult, ALU.mult).then_inc(om_ready.sem, 1)
                eng.wait_ge(z_evac.sem, z_evac.at(l, 20))
                tt(b_p, b_c, b_h, ALU.mult)
                eng.drain()
                cv, pp = blocks(b_cv, 4), blocks(b_p, 4)
                for b in range(4):
                    ts(cv[:, b, :], pp[:, b, :], column(l, "conv_b_w", 8 + b), None, ALU.mult)
                for d in range(1, 3):
                    eng.drain()
                    for b in range(4):
                        eng.scalar_tensor_tensor(cv[:, b, d:T], pp[:, b, 0:T - d], column(l, "conv_b_w", (2 - d) * 4 + b),
                                                 cv[:, b, d:T], ALU.mult, ALU.add)
                eng.wait_ge(mult_ready.sem, mult_ready.at(l, 1))
                tt(r_i, r_i, r_t, ALU.mult)
                eng.drain()
                for b in range(4):
                    sl = slice(b * T, b * T + T)
                    eng.tensor_tensor_scan(r_u[:, sl], r_r[:, sl], r_i[:, sl], 0.0, ALU.mult, ALU.add)
                eng.memset(wr[:, :, NR:32], 0.0)
                eng.drain()
                tt(mixT[:, 0:4, :].rearrange("p k t -> p (k t)"), r_u, r_g, ALU.mult).then_inc(lru_done.sem, 1)
                def rest_of_w(c, n, i):
                    s = N_IN + c
                    eng.wait_ge(w_rounded.sem, w_rounded.at(l, 2 * c + n + 1))
                    tt(ring_lo[:, s % SLOTS, 8 * i:8 * i + 8, :], slab(s % SLOTS)[:, 8 * i:8 * i + 8, :],
                       w_hi[i][:].bitcast(F32), ALU.subtract).then_inc(w_split.sem, 1)

                eng.wait_ge(mix_rounded.sem, mix_rounded.at(l, 1))
                tt(mix_lo[:, 0:4, :], mixT[:, 0:4, :], mix_hi[:, 0:4, :].bitcast(F32), ALU.subtract)
                tt(mix_lo[:, 8:16, :], mixT[:, 8:16, :], mix_hi[:, 8:16, :].bitcast(F32), ALU.subtract
                   ).then_inc(mix_split.sem, 1)
                rest_of_w(0, 0, 1)
                for i in range(2):
                    eng.wait_ge(acc_full.sem, acc_full.at(l, 21 + i))
                    tt(mixT[:, 4 + 2 * i:6 + 2 * i, :].rearrange("p k t -> p (k t)"), b_cv[:, i * 512:i * 512 + 512],
                       ps[:, i, :], ALU.mult).then_inc(mixb_ready.sem, 1)

                eng.wait_ge(mix_rounded.sem, mix_rounded.at(l, 2))
                tt(mix_lo[:, 4:8, :], mixT[:, 4:8, :], mix_hi[:, 4:8, :].bitcast(F32), ALU.subtract
                   ).then_inc(mix_split.sem, 1)
                rest_of_w(0, 1, 0)

                eng.wait_ge(h_ready, (2 * l + 1) * NT)
                for c in range(N_OUT):
                    if c + 1 < N_OUT:
                        rest_of_w(c + 1, 0, 1)
                    for t in range(NT):
                        eng.wait_ge(acc_full.sem, acc_full.at(l, 2 * (N_IN + c) + t + 1))
                        sl = h[:, t, c * 512:c * 512 + 512]
                        eng.scalar_tensor_tensor(sl, sl, ALPHA, ps[:, 2 + 2 * (c % 2) + t, :], ALU.mult, ALU.add
                                                 ).then_inc(res_add.sem, 1)
                        eng.drain()
                        eng.bn_stats(stats[:, t, c, :], sl)
                    if c + 1 < N_OUT:
                        rest_of_w(c + 1, 1, 0)
                norm(2 * l + 1, cur_ln[:, 0])

                eng.wait_ge(router_loaded.sem, router_loaded.at(l, 64))
                eng.wait_ge(logits_done.sem, logits_done.at(l, 1))
                tt(lg, ps[:, 2, 0:NT * NR].rearrange("p (t n) -> p t n", t=NT),
                   br.rearrange("p (o n) -> p o n", o=1).to_broadcast([P, NT, NR]), ALU.add)
                eng.drain()

                def first_of(dst, vals, top):
                    eng.tensor_reduce(top, vals, AX.X, ALU.max)
                    eng.drain()
                    tt(rk, vals, top.to_broadcast([P, NT, 4]), ALU.is_equal)
                    eng.drain()
                    tt(rk, rk, desc[:].rearrange("p (o n) -> p o n", o=1).to_broadcast([P, NT, 4]), ALU.mult)
                    eng.drain()
                    eng.tensor_reduce(rkm, rk, AX.X, ALU.max)
                    eng.drain()
                    tt(dst, rk, rkm.to_broadcast([P, NT, 4]), ALU.is_equal)
                    eng.drain()

                first_of(goh, lg[:, :, 0:G], gmax)
                tt(ex[:, :, 0:4], lg[:, :, 0:G], gmax.to_broadcast([P, NT, 4]), ALU.subtract)
                for g in range(G):
                    tt(t16[:, :, 4 * g:4 * g + 4], lg[:, :, G + 4 * g:G + 4 * g + 4],
                       goh[:, :, g:g + 1].to_broadcast([P, NT, 4]), ALU.mult)
                eng.drain()
                eng.tensor_reduce(eg, t16.rearrange("p t (g e) -> p t e g", g=4), AX.X, ALU.add)
                eng.drain()
                first_of(oh[:, 0], eg, emax[:, 0])
                eng.scalar_tensor_tensor(eg, oh[:, 0], -BIG, eg, ALU.mult, ALU.add)
                eng.drain()
                first_of(oh[:, 1], eg, emax[:, 1])
                tt(ex[:, :, 4:5], emax[:, 1], emax[:, 0], ALU.subtract).then_inc(ex_in.sem, 1)
                for i in range(2):
                    for g in range(G):
                        tt(M[:, i, :, 4 * g:4 * g + 4], oh[:, i], goh[:, :, g:g + 1].to_broadcast([P, NT, 4]), ALU.mult)
                eng.drain()
                tt(M[:, 2], M[:, 0], M[:, 1], ALU.add).then_inc(m_ready.sem, 1)
                eng.wait_ge(ex_ready.sem, ex_ready.at(l, 1))
                eng.tensor_reduce(gval, ex[:, :, 0:4], AX.X, ALU.add)
                ts(wts[:, 1], ex[:, :, 4:5], 1.0, None, ALU.add)
                eng.drain()
                tt(gval, gval, wts[:, 1], ALU.mult)
                eng.drain()
                eng.reciprocal(wts[:, 0], gval)
                eng.drain()
                tt(wts[:, 1], wts[:, 0], ex[:, :, 4:5], ALU.mult)
                eng.wait_ge(ranks_done.sem, ranks_done.at(l, 1))
                eng.tensor_copy(tab[:, 0, :], ps[:, 1, 32:48])
                eng.drain()
                ts(tab[:, 1, :], tab[:, 0, :], float(BLK), 1.0, ALU.is_gt, ALU.add)
                for lim in range(2 * BLK, T, BLK):
                    eng.drain()
                    eng.scalar_tensor_tensor(tab[:, 1, :], tab[:, 0, :], float(lim), tab[:, 1, :], ALU.is_gt, ALU.add)
                eng.drain()
                for i in range(2):
                    eng.tensor_tensor_scan(scn[:, i, :], tab[:, i, :], tab[:, i, :], 0.0 if i == 0 else carry[:],
                                           ALU.add, ALU.bypass)
                eng.drain()
                tt(tab[:, 0, :], scn[:, 0, :], tab[:, 0, :], ALU.subtract)
                tt(tab[:, 2, :], scn[:, 1, :], tab[:, 1, :], ALU.subtract)
                eng.tensor_copy(carry[:], scn[:, 1, 15:16])
                eng.drain()
                eng.tensor_copy(tabi[:, 0:3, :], tab).then_inc(tab_ready.sem, 1)
                for t in range(NT):
                    tt(pos[:, t, :], ps[:, 1, 16 * t:16 * t + 16], tab[:, 0, :], ALU.add)
                eng.drain()
                for i in range(2):
                    tt(t16, M[:, i], pos, ALU.mult)
                    eng.drain()
                    eng.tensor_reduce(pos12[:, i], t16, AX.X, ALU.add)
                    eng.drain()
                for t in range(NT):
                    ts(hot[:, t, :], slot_iota[:], pos12[:, 0, t, :], None, ALU.is_equal)
                eng.drain()
                for t in range(NT):
                    last = eng.scalar_tensor_tensor(hot[:, t, :], slot_iota[:], pos12[:, 1, t, :], hot[:, t, :],
                                                    ALU.is_equal, ALU.add)
                last.then_inc(hot_ready.sem, 1)
                eng.memset(xgT[:, :, S:SP_], 0.0)
                ht = area(46, 512)
                for t in range(NT):
                    ts(hotw[:, t, :], slot_iota[:], pos12[:, 0, t, :], wts[:, 0, t, :], ALU.is_equal, ALU.mult)
                    ts(ht, slot_iota[:], pos12[:, 1, t, :], wts[:, 1, t, :], ALU.is_equal, ALU.mult)
                    eng.drain()
                    tt(hotw[:, t, :], hotw[:, t, :], ht, ALU.add)
                    eng.drain()
                for k in range(1, KD, 2):
                    eng.wait_ge(gath_done.sem, gath_done.at(l, k + 1))
                    ts(xgT[:, k, 0:S], ps[:, k % 8, :], cur_ln[:, 0, 0, k:k + 1],
                       cur_ln[:, 0, 1, k:k + 1], ALU.mult, ALU.add).then_inc(gath_dve.sem, 1)

                eng.drain()
                with eng.Fori(0, E) as e:
                    first, n, g0 = expert_row(eng, 0, e), expert_row(eng, 1, e), expert_row(eng, 2, e)
                    with eng.Fori(0, n) as j:
                        eng.wait_ge(gu_done, g0 + j + 1)
                        eng.wait_ge(gath_act.sem, gath_act.at(l, KD // 2))
                        eng.tensor_scalar(xe, xgT[:, :, bass.ds(block_start(first, j), BLK)], 1.0, None, ALU.mult
                                          ).then_inc(xe_ready, 1)
                        eng.wait_ge(sg_ready, g0 + j + 1)
                        tt(hmid, sgate, ps[:, 0, 256:512], ALU.mult).then_inc(hm_ready, 1)

                for c in range(1, 16, 2):
                    eng.wait_ge(yS_done.sem, yS_done.at(l, c + 1))
                    eng.tensor_copy(ySort[:, c // 4, (c % 4) * 512:(c % 4) * 512 + 512], ps[:, c % 8, :]
                                    ).then_inc(yS_dve.sem, 1)
                eng.wait_ge(h_ready, (2 * l + 2) * NT)
                for c in range(N_OUT):
                    for t in range(NT):
                        eng.wait_ge(sc_done.sem, sc_done.at(l, 2 * c + t + 1))
                        sl = h[:, t, c * 512:c * 512 + 512]
                        eng.scalar_tensor_tensor(sl, sl, ALPHA, ps[:, 2 * c + t, :], ALU.mult, ALU.add)
                        eng.drain()
                        eng.bn_stats(stats[:, t, c, :], sl)
                norm(2 * l + 2, cur_ln[:, 1])
                affine_h(gb2_loaded.sem, gb2_loaded.at(l, 32))
                eng.drain()


_INS = ['x', 'ln0_g', 'ln0_b', 'w_in', 'conv_a_w', 'conv_a_b', 'lru_wa', 'lru_ba', 'lru_wx', 'lru_bx', 'lru_lam',
        'conv_b_w', 'gla_wa2', 'gla_ba2', 'gla_norm_w', 'att_rel_bias', 'w_out', 'ln1_g', 'ln1_b', 'w_rg', 'b_rg',
        'w_re', 'b_re', 'w_gate', 'w_up', 'w_down', 'ln2_g', 'ln2_b']


def kernel(**inputs):
    import numpy as _np
    import concourse.bacc as _bacc
    from concourse import mybir as _mybir
    from concourse.bass_utils import run_bass_kernel_spmd as _run

    nc = _bacc.Bacc("TRN2", target_bir_lowering=False, num_devices=1)
    arrays, args = {}, []
    for name in _INS:
        a = _np.ascontiguousarray(inputs[name])
        arrays[f"in_{name}_dram"] = a
        args.append(nc.dram_tensor(f"in_{name}_dram", a.shape, _mybir.dt.from_np(a.dtype), kind="ExternalInput").ap())
    args.append(nc.dram_tensor("out_0_dram", inputs["x"].shape, _mybir.dt.float32, kind="ExternalOutput").ap())
    trunk(nc, *args)
    r = _run(nc, [arrays], core_ids=[0])
    return r.results[0]["out_0_dram"]
```
